# Optimizing a Trainium2 kernel written in Bass

```python
import math
import jax, jax.numpy as jnp
from jax import lax
import numpy as np

D_MODEL = 1024
BATCH = 1
SEQ = 256
DEPTH = 2

CHUNK = 64
Q_BLOCK = 128
SPARSE_Q_BLOCK = 64
D_MIX = D_MODEL
D_A = D_MIX // 2
D_B = D_MIX - D_A
HEAD_DIM = 64
A_HEADS = D_A // HEAD_DIM
B_HEADS = D_B // (2 * HEAD_DIM)
B_VDIM = 2 * HEAD_DIM
IDX_HEADS = 4
IDX_DIM = 64
TOPK_MAX = 256
ROPE_THETA = 500000.0
ROT_DIM = HEAD_DIM // 4
EPS = 1e-6
D_PLE = 256
NEG_INF = -1e30
D_IN = 3 * D_A + IDX_HEADS * IDX_DIM + IDX_DIM + IDX_HEADS + D_A + 4 * D_B

kernel_name = "hybrid_dsa_diffattn_sandwich_ple"

def _rmsnorm(x, g):
    x32 = x.astype(jnp.float32)
    y = x32 * lax.rsqrt(jnp.mean(x32 * x32, axis=-1, keepdims=True) + EPS)
    return (y * g.astype(jnp.float32)).astype(x.dtype)

def _rope_tables(seq, dtype):
    pos = jnp.arange(seq, dtype=jnp.float32)
    inv = ROPE_THETA ** (-jnp.arange(0, ROT_DIM, 2, dtype=jnp.float32) / ROT_DIM)
    ang = pos[:, None] * inv[None, :]
    return jnp.cos(ang).astype(dtype), jnp.sin(ang).astype(dtype)

def _partial_rope(x, cos, sin):
    half = ROT_DIM // 2
    x1 = x[..., :half]
    x2 = x[..., half:ROT_DIM]
    c = cos[None, :, None, :]
    s = sin[None, :, None, :]
    return jnp.concatenate([x1 * c - x2 * s, x2 * c + x1 * s, x[..., ROT_DIM:]], axis=-1)

def _to_blocks(a, blk):
    b, s = a.shape[:2]
    return a.reshape((b, s // blk, blk) + a.shape[2:]).swapaxes(0, 1)

def _from_blocks(a):
    nb, b, blk = a.shape[:3]
    return a.swapaxes(0, 1).reshape((b, nb * blk) + a.shape[3:])

def _split_in(z):
    sizes = (D_A, D_A, D_A, IDX_HEADS * IDX_DIM, IDX_DIM, IDX_HEADS, D_A,
             B_HEADS * 2 * HEAD_DIM, B_HEADS * 2 * HEAD_DIM, B_HEADS * B_VDIM, D_B)
    offs = [int(o) for o in np.cumsum(sizes)[:-1]]
    return jnp.split(z, offs, axis=-1)

def _dsa_attention(q, k, v, qi, ki, wi, top_k):
    seq = q.shape[1]
    spos = jnp.arange(seq, dtype=jnp.int32)
    ki32 = ki.astype(jnp.float32)

    def block(args):
        qb, qib, wib, tpos = args
        limit = (tpos // CHUNK + 1) * CHUNK
        dots = jnp.einsum('bqhd,bsd->bqhs', qib.astype(jnp.float32), ki32) * (IDX_DIM ** -0.5)
        iscore = jnp.einsum('bqhs,bqh->bqs', jax.nn.relu(dots), wib.astype(jnp.float32))
        adm = spos[None, :] < limit[:, None]
        iscore = jnp.where(adm[None], iscore, -jnp.inf)
        _, idx = lax.top_k(iscore, top_k)
        valid = idx < limit[None, :, None]
        kg = jax.vmap(lambda kk, ii: kk[ii])(k, idx)
        vg = jax.vmap(lambda vv, ii: vv[ii])(v, idx)
        logits = jnp.einsum('bqhd,bqkhd->bhqk', qb, kg).astype(jnp.float32) * (HEAD_DIM ** -0.5)
        logits = jnp.where(valid[:, None], logits, NEG_INF)
        probs = jax.nn.softmax(logits, axis=-1).astype(v.dtype)
        return jnp.einsum('bhqk,bqkhd->bqhd', probs, vg)

    out = lax.map(block, (_to_blocks(q, SPARSE_Q_BLOCK), _to_blocks(qi, SPARSE_Q_BLOCK),
                          _to_blocks(wi, SPARSE_Q_BLOCK), spos.reshape(-1, SPARSE_Q_BLOCK)))
    out = _from_blocks(out)
    return out.reshape(out.shape[0], seq, -1)

def _diff_attention(q, k, v, lam, lam_init, sub_g):
    seq = q.shape[1]
    spos = jnp.arange(seq, dtype=jnp.int32)
    schunk = spos // CHUNK

    def block(args):
        qb, tpos = args
        allowed = schunk[None, :] <= (tpos // CHUNK)[:, None]
        logits = jnp.einsum('bqhcd,bshcd->bchqs', qb, k).astype(jnp.float32) * (HEAD_DIM ** -0.5)
        logits = jnp.where(allowed, logits, NEG_INF)
        probs = jax.nn.softmax(logits, axis=-1)
        attn = (probs[:, 0] - lam * probs[:, 1]).astype(v.dtype)
        return jnp.einsum('bhqs,bshe->bqhe', attn, v)

    out = _from_blocks(lax.map(block, (_to_blocks(q, Q_BLOCK), spos.reshape(-1, Q_BLOCK))))
    out = _rmsnorm(out, sub_g) * (1.0 - lam_init)
    return out.reshape(out.shape[0], seq, -1)

def setup_inputs(seed: int = 0) -> dict:
    key = jax.random.key(seed)
    ks = jax.random.split(key, 14)
    f32 = jnp.float32

    def nrm(k, shape, scale):
        return jax.random.normal(k, shape, f32) * scale

    return {
        "x": nrm(ks[0], (BATCH, SEQ, D_MODEL), 1.0),
        "p": nrm(ks[1], (DEPTH, BATCH, SEQ, D_PLE), 1.0),
        "pre_norm_g": 1.0 + nrm(ks[2], (DEPTH, D_MODEL), 0.02),
        "w_in": nrm(ks[3], (DEPTH, D_MODEL, D_IN), D_MODEL ** -0.5),
        "w_out": nrm(ks[4], (DEPTH, D_MIX, D_MODEL), D_MIX ** -0.5),
        "post_norm_g": 1.0 + nrm(ks[5], (DEPTH, D_MODEL), 0.02),
        "lambda_q1": nrm(ks[6], (DEPTH, HEAD_DIM), 0.1),
        "lambda_k1": nrm(ks[7], (DEPTH, HEAD_DIM), 0.1),
        "lambda_q2": nrm(ks[8], (DEPTH, HEAD_DIM), 0.1),
        "lambda_k2": nrm(ks[9], (DEPTH, HEAD_DIM), 0.1),
        "subln_g": 1.0 + nrm(ks[10], (DEPTH, B_VDIM), 0.02),
        "w_ple_gate": nrm(ks[11], (DEPTH, D_MODEL, D_MODEL), D_MODEL ** -0.5),
        "w_ple_proj": nrm(ks[12], (DEPTH, D_PLE, D_MODEL), D_PLE ** -0.5),
        "ple_norm_g": 1.0 + nrm(ks[13], (DEPTH, D_MODEL), 0.02),
    }

def reference(x, p, pre_norm_g, w_in, w_out, post_norm_g, lambda_q1, lambda_k1, lambda_q2,
              lambda_k2, subln_g, w_ple_gate, w_ple_proj, ple_norm_g):
    bsz, seq, _ = x.shape
    top_k = min(TOPK_MAX, seq // 4)
    cos, sin = _rope_tables(seq, x.dtype)
    for i in range(DEPTH):
        h = _rmsnorm(x, pre_norm_g[i])
        z = h @ w_in[i]
        qa, ka, va, qi, ki, wi, ga, qb, kb, vb, gb = _split_in(z)
        qa = _partial_rope(qa.reshape(bsz, seq, A_HEADS, HEAD_DIM), cos, sin)
        ka = _partial_rope(ka.reshape(bsz, seq, A_HEADS, HEAD_DIM), cos, sin)
        va = va.reshape(bsz, seq, A_HEADS, HEAD_DIM)
        qi = _partial_rope(qi.reshape(bsz, seq, IDX_HEADS, IDX_DIM), cos, sin)
        ki = _partial_rope(ki[:, :, None, :], cos, sin)[:, :, 0, :]
        wi = wi * (IDX_HEADS ** -0.5)
        oa = _dsa_attention(qa, ka, va, qi, ki, wi, top_k)
        qb = _partial_rope(qb.reshape(bsz, seq, B_HEADS * 2, HEAD_DIM), cos, sin).reshape(bsz, seq, B_HEADS, 2, HEAD_DIM)
        kb = _partial_rope(kb.reshape(bsz, seq, B_HEADS * 2, HEAD_DIM), cos, sin).reshape(bsz, seq, B_HEADS, 2, HEAD_DIM)
        vb = vb.reshape(bsz, seq, B_HEADS, B_VDIM)
        lam_init = 0.8 - 0.6 * math.exp(-0.3 * i)
        lam = (jnp.exp(jnp.sum(lambda_q1[i].astype(jnp.float32) * lambda_k1[i].astype(jnp.float32)))
               - jnp.exp(jnp.sum(lambda_q2[i].astype(jnp.float32) * lambda_k2[i].astype(jnp.float32)))
               + lam_init)
        ob = _diff_attention(qb, kb, vb, lam, lam_init, subln_g[i])
        y = jnp.concatenate([oa * jax.nn.silu(ga), ob * jax.nn.silu(gb)], axis=-1) @ w_out[i]
        x = x + _rmsnorm(y, post_norm_g[i])
        gate = jax.nn.sigmoid(x @ w_ple_gate[i])
        e = (p[i] @ w_ple_proj[i]) * gate
        x = x + _rmsnorm(e, ple_norm_g[i])
    return x


_drawn_inputs = setup_inputs


def setup_inputs(seed=0):
    import zlib

    import numpy as np

    out = dict(_drawn_inputs(seed))
    spreads = {}
    factors = {}
    for name, (base, spread) in spreads.items():
        noise = np.random.default_rng([zlib.crc32(name.encode()), seed]).standard_normal(out[name].shape)
        drawn = base * np.exp(spread * noise) if base else spread * noise
        out[name] = __import__('jax').numpy.asarray(drawn.astype(out[name].dtype))
    for name, factor in factors.items():
        out[name] = (out[name] * factor).astype(out[name].dtype)
    return out
```

```python
import math
from contextlib import ExitStack

import concourse.bass as bass
from concourse import mybir

DEPTH, SEQ, D_MODEL, D_PLE = 2, 256, 1024, 256
P = 128
NB = SEQ // P
KT = D_MODEL // P
HEAD = 64
CHUNK = 64
TOPK = min(256, SEQ // 4)
D_HALF = D_MODEL // 2
A_HEADS, B_HEADS, IDX_HEADS = 8, 4, 4
ROT = HEAD // 4
EPS = 1e-6
NEG = -1e30
INADMISSIBLE = -1e38
TAKEN = -3e38
IDX_W = IDX_HEADS * HEAD + HEAD + IDX_HEADS
N = 512

_sizes = [D_HALF, D_HALF, D_HALF, IDX_HEADS * HEAD, HEAD, IDX_HEADS, D_HALF, D_HALF, D_HALF, D_HALF, D_HALF]
_off = [sum(_sizes[:i]) for i in range(len(_sizes))]
COL = dict(QA=_off[0], KA=_off[1], VA=_off[2], IDX=_off[3], GA=_off[6], QB=_off[7], KB=_off[8], VB=_off[9],
           GB=_off[10])

KU = 2
IN_CHUNKS = ["IDX", "QB", "KB", "VB", "QA", "KA", "VA", "GA", "GB"]
UNITS = [("PLE", n, 0, KU, N) for n in range(2)]
for _c in IN_CHUNKS:
    UNITS += [(_c, 0, k, KU, IDX_W if _c == "IDX" else N) for k in range(0, KT, KU)]
for _c in ("WO", "WG"):
    UNITS += [(_c, n, k, KU, N) for n in range(2) for k in range(0, KT, KU)]
U = len(UNITS)
FIRST = {}
for _i, _u in enumerate(UNITS):
    FIRST.setdefault(_u[0], _i)
LAST_OF = {(_u[0], _u[1]): _i for _i, _u in enumerate(UNITS)}
UQ = KT // KU
B0_ORDER = [("PLE", 0), ("PLE", 1)] + [(c, 0) for c in IN_CHUNKS] + [("WO", 0), ("WO", 1), ("WG", 0), ("WG", 1)]
RAW_SLOTS, SLOTS = 5, 9
UE = KU * N


def layer_steps(L):
    out = []

    def mms(chunk, order, side):
        for i, (u, b) in enumerate(order):
            out.append(("mm", FIRST[chunk] + u, b))
            out.extend(side.get(i, ()))

    both = [(u, b) for u in range(UQ) for b in range(NB)]
    one = lambda b, n=UQ: [(u, b) for u in range(n)]
    if L == 0:
        out += [("pT",), ("pre", 0), ("pre", 1)]
        mms("PLE", [(n, b) for n in range(2) for b in range(NB)], {})
    else:
        mms("PLE", [(n, b) for n in range(2) for b in range(NB)],
            {0: [("ple0", 1, L - 1)], 1: [("ple1", 1, L - 1)], 3: [("pre", 1)]})
    out += [("t8", "h", 0, 0), ("t8", "h", 0, 1)]
    mms("IDX", one(0), {})
    mms("QB", one(0), {1: [("t8", "h", 1, 0), ("t8", "h", 1, 1)]})
    mms("IDX", one(1), {})
    mms("QB", one(1), {1: [("TI", 0)], 2: [("D", 0)], 3: [("D", 1)]})
    kb = {i: [("topk", 0, i)] for i in range(8)}
    kb[0] = [("TI", 1)] + kb[0]
    kb[1] = [("T", "QB", 0)] + kb[1]
    kb[2] = [("D", 2)] + kb[2]
    kb[3] = [("D", 3)] + kb[3]
    kb[4] = [("T", "QB", 1)] + kb[4]
    mms("KB", both, kb)
    vb = {i: [("topk", 1, i)] for i in range(8)}
    vb[2] = [("T", "KB", 0)] + vb[2]
    vb[3] = [("S", 0)] + vb[3]
    vb[4] = [("T", "KB", 1), ("S", 1)] + vb[4]
    vb[5] = [("S", 2)] + vb[5]
    vb[6] = [("S", 3)] + vb[6]
    vb[7] = [("PT", 0)] + vb[7]
    mms("VB", both, vb)
    mms("QA", both, {0: [("S", 4)], 1: [("S", 5)], 2: [("PV", 0)], 3: [("PT", 1)], 4: [("PV", 1)], 5: [("PT", 2)],
                     6: [("PV", 2)]})
    mms("KA", both, {2: [("T", "QA", 0)], 4: [("T", "QA", 1)]})
    mms("VA", both, {2: [("T", "KA", 0)], 3: [("S", 6)], 4: [("T", "KA", 1), ("S", 7)], 5: [("S", 8), ("PT", 3)],
                     6: [("S", 9), ("PT", 4)], 7: [("S", 10)]})
    mms("GA", both, {0: [("PT", 5), ("S", 11)], 1: [("PV", 3), ("PT", 6)], 2: [("PV", 4), ("PT", 7)],
                     3: [("PV", 5), ("PT", 8)], 4: [("PV", 6)], 5: [("PV", 7)], 6: [("PV", 8)]})
    mms("GB", one(0), {})
    mms("GB", one(1), {1: [("t8", "y", 0, 0), ("t8", "y", 0, 1)]})
    mms("WO", one(0, 2 * UQ), {4: [("t8", "y", 1, 0), ("t8", "y", 1, 1)]})
    wo1 = {0: [("post0", 0)], 1: [("post1", 0)], 5: [("t8", "x", 0, 0), ("t8", "x", 0, 1)]}
    if L + 1 < DEPTH:
        wo1[2] = [("pT",)]
    mms("WO", one(1, 2 * UQ), wo1)
    mms("WG", one(0, 2 * UQ), {0: [("post0", 1)], 1: [("post1", 1)], 5: [("t8", "x", 1, 0), ("t8", "x", 1, 1)]})
    mms("WG", one(1, 2 * UQ), {0: [("ple0", 0, L)], 2: [("ple1", 0, L)],
                               4: [("pre", 0, L + 1)] if L + 1 < DEPTH else []})
    if L + 1 == DEPTH:
        out += [("ple0", 1, L), ("ple1", 1, L)]
    return out


def all_steps():
    steps = [(L, s) for L in range(DEPTH) for s in layer_steps(L)]
    last_use = {}
    for pos, (L, s) in enumerate(steps):
        if s[0] == "mm":
            last_use[L * U + s[1]] = pos
    splits = [[] for _ in steps]
    for g in range(DEPTH * U):
        splits[0 if g < SLOTS else last_use[g - SLOTS] + 2].append(g)
    return steps, splits


def build(nc, x, p, pre_norm_g, w_in, w_out, post_norm_g, lambda_q1, lambda_k1, lambda_q2, lambda_k2, subln_g,
          w_ple_gate, w_ple_proj, ple_norm_g, rope, out):
    fp32, f32r, bf16 = mybir.dt.float32, mybir.dt.float32r, mybir.dt.bfloat16
    ALU, ACT, AX = mybir.AluOpType, mybir.ActivationFunctionType, mybir.AxisListType
    STEPS, SPLITS = all_steps()

    ctx = ExitStack()
    with ctx:
        def sb(name, shape, dt=fp32):
            return ctx.enter_context(nc.sbuf_tensor(name, shape, dt))

        def sem(name):
            return ctx.enter_context(nc.semaphore(name))

        raw = sb("raw", [P, RAW_SLOTS, UE])
        w_hi = sb("w_hi", [P, SLOTS, UE], f32r)
        w_lo = sb("w_lo", [P, SLOTS, UE], f32r)
        resid = sb("resid", [P, NB, D_MODEL])
        work = sb("work", [P, NB, D_MODEL])
        act_hi = sb("act_hi", [P, NB, KT, P], f32r)
        act_lo = sb("act_lo", [P, NB, KT, P], f32r)
        p_raw = sb("p_raw", [P, NB, D_PLE])
        p_hi = sb("p_hi", [P, NB, D_PLE // P, P], f32r)
        p_lo = sb("p_lo", [P, NB, D_PLE // P, P], f32r)
        emb = sb("emb", [P, NB, D_MODEL])
        v_all = sb("v_all", [P, NB, 2, D_HALF])
        z_idx = v_all[:, :, 0, 0:6 * HEAD]
        gate = sb("gate", [P, NB, D_HALF])
        qT = [sb("qT_b", [P, 4, SEQ]), sb("qT_a", [P, 4, SEQ])]
        kT = [sb("kT_b", [P, 4, SEQ]), sb("kT_a", [P, 4, SEQ])]
        y_mix = [qT[g][:, :, :].rearrange("p j t -> p (j t)").rearrange("p (b n) -> p b n", b=NB) for g in range(2)]
        probs = sb("probs", [P, 4, N])
        pT = sb("pT", [P, 3, 4, P])
        idxT = pT[:, 0:2, :, :].rearrange("p a t q -> p (a t q)")[:, 0:3 * SEQ].rearrange("p (j t) -> p j t", j=3)
        score = [sb("score0", [P, P]), sb("score1", [P, SEQ])]
        sel_mask = [sb("sel_mask0", [P, P], bf16), sb("sel_mask1", [P, SEQ], bf16)]
        causal = sb("causal", [P, SEQ], bf16)
        ident = sb("ident", [P, P])
        ident16 = sb("ident16", [P, P], bf16)
        junk = sb("junk", [P, D_MODEL], bf16)
        g_pre = sb("g_pre", [P, D_MODEL])
        g_post = sb("g_post", [P, D_MODEL])
        g_ple = sb("g_ple", [P, D_MODEL])
        g_sub = sb("g_sub", [P, P])
        g_subs = sb("g_subs", [P, P])
        lam_in = sb("lam_in", [P, 4, HEAD])
        lam_prod = sb("lam_prod", [P, 2, HEAD])
        lam_s = sb("lam_s", [P, 2])
        lam_e = sb("lam_e", [P, 2])
        neg_lam = sb("neg_lam", [P, 1])
        cos2 = sb("cos2", [P, NB, ROT])
        sin2 = sb("sin2", [P, NB, ROT])
        rot_a = sb("rot_a", [P, 8, ROT])
        rot_b = sb("rot_b", [P, 8, ROT])
        w_idx = sb("w_idx", [P, NB, IDX_HEADS])
        top8 = sb("top8", [P, 8])
        neg_max = sb("neg_max", [P, 2, 4])
        row_sum = sb("row_sum", [P, 2, NB, 8])
        row_rec = sb("row_rec", [P, 2, NB, 8])
        mix_c = sb("mix_c", [P, 4])
        ssq = sb("ssq", [P, 3, NB, 2])
        var = sb("var", [P, 3, NB])
        rstd = sb("rstd", [P, 3, NB])
        ssq_h = sb("ssq_h", [P, NB, B_HEADS])
        var_h = sb("var_h", [P, NB, B_HEADS])
        rstd_h = sb("rstd_h", [P, NB, B_HEADS])
        scale_h = sb("scale_h", [P, NB, B_HEADS])
        minus_half = sb("minus_half", [P, B_HEADS])

        proj = [ctx.enter_context(nc.psum_tensor(f"proj{i}", [P, N], fp32)) for i in range(4)]
        sc = [ctx.enter_context(nc.psum_tensor(f"sc{i}", [P, N], fp32)) for i in range(2)]
        tr = ctx.enter_context(nc.psum_tensor("tr", [P, N], fp32))
        pv = ctx.enter_context(nc.psum_tensor("pv", [P, N], fp32))

        raw_in = [sem(f"raw_in{i}") for i in range(RAW_SLOTS)]
        hi_done, lo_done = sem("hi_done"), sem("lo_done")
        unit_used = sem("unit_used")
        b0_done = sem("b0_done")
        x_in = [sem(f"x_in{b}") for b in range(NB)]
        rope_in, p_in, gpre_in, gpost_in, gple_in, small_in = (
            sem(n) for n in ("rope_in", "p_in", "gpre_in", "gpost_in", "gple_in", "small_in"))
        const_done = sem("const_done")
        sq_done = [sem(f"sq_done{i}") for i in range(3)]
        var_done = [sem(f"var_done{i}") for i in range(3)]
        rstd_done = [sem(f"rstd_done{i}") for i in range(3)]
        h_done, x1_done, x2_done = sem("h_done"), sem("x1_done"), sem("x2_done")
        t8_done, at_hi, at_lo = sem("t8_done"), sem("at_hi"), sem("at_lo")
        ptr_done, p_hi_done, p_lo_done = sem("ptr_done"), sem("p_hi_done"), sem("p_lo_done")
        ple_out = sem("ple_out")
        idx_out, z_out, v_out = sem("idx_out"), sem("z_out"), sem("v_out")
        rope_idx, rope_z = sem("rope_idx"), sem("rope_z")
        tr_done, tr_out = sem("tr_done"), sem("tr_out")
        dots_done, relu_done, score_done = sem("dots_done"), sem("relu_done"), sem("score_done")
        mask_done = sem("mask_done")
        s_done, max_done, exp_done, mix_done = (sem(n) for n in ("s_done", "max_done", "exp_done", "mix_done"))
        pv_done, pv_out = sem("pv_done"), sem("pv_out")
        sqh_done, varh_done, rstdh_done = sem("sqh_done"), sem("varh_done"), sem("rstdh_done")
        sig_done, glu_done, y_done = sem("sig_done"), sem("glu_done"), sem("y_done")
        wo_scaled, wg_sig, e_done = sem("wo_scaled"), sem("wg_sig"), sem("e_done")
        lam_sum, lam_exp, lam_done = sem("lam_sum"), sem("lam_exp"), sem("lam_done")
        dve_chain, pool_chain = sem("dve_chain"), sem("pool_chain")
        stored = sem("stored")

        def bank_of(chunk, n, b):
            if chunk == "PLE":
                return 2 * (1 - n) + b
            if chunk in ("WO", "WG"):
                return (2 if b == 0 else 0) + n
            return 2 * (IN_CHUNKS.index(chunk) % 2) + b

        def wait_sum(eng, L, chunk, n, b):
            if b == 0:
                eng.wait_ge(b0_done, L * len(B0_ORDER) + B0_ORDER.index((chunk, n)) + 1)
            else:
                eng.wait_ge(unit_used, L * U + LAST_OF[chunk, n] + 1)

        Z_ORDER = ["QB", "KB", "QA", "KA"]

        def z_view(chunk, b):
            half = Z_ORDER.index(chunk) % 2
            return work[:, b, half * N:(half + 1) * N]

        tr_steps = [s for s in layer_steps(0) if s[0] in ("TI", "T", "PT")]
        TRN = len(tr_steps)

        def tr_index(L, s):
            return L * TRN + tr_steps.index(s) + 1

        def s_task(i):
            g, r = divmod(i, 6)
            if r < 2:
                return g, 0, list(range(r, 8, 2)), P
            q, odd = divmod(r - 2, 2)
            return g, 1, [4 * q + odd, 4 * q + odd + 2], SEQ

        def pt_task(n):
            si = [0, 2, 4, 6, 7, 8, 9, 10, 11][n]
            g, b, maps, keys = s_task(si)
            return g, b, [(m // 2 if g == 0 else m, kt, si, j * keys + kt * P)
                          for j, m in enumerate(maps) for kt in range(b + 1)]

        PT_OF_S = {}
        for n_ in range(9):
            for _, _, s_, _ in pt_task(n_)[2]:
                PT_OF_S[s_] = n_
        PV_GROUP = [(0, 0, [0]), (0, 1, [1, 2]), (1, 0, [3, 4]), (1, 1, [5, 6, 7, 8])]

        T8_BASE = dict(h=0, y=4, x=8)

        def t8_index(kind, b, half):
            return T8_BASE[kind] + 2 * b + half

        block = ctx.enter_context(nc.Block())

        @block.sync
        def _(sp):
            for b in range(NB):
                sp.dma_start(resid[:, b, :], x[0, b * P:(b + 1) * P, :]).then_inc(x_in[b], 16)
            for g in range(DEPTH * U):
                L, u = divmod(g, U)
                chunk, n, k0, nk, cols = UNITS[u]
                if chunk == "PLE":
                    src = w_ple_proj[L, :, n * N:(n + 1) * N]
                elif chunk == "WO":
                    src = w_out[L, k0 * P:(k0 + nk) * P, n * N:(n + 1) * N]
                elif chunk == "WG":
                    src = w_ple_gate[L, k0 * P:(k0 + nk) * P, n * N:(n + 1) * N]
                else:
                    src = w_in[L, k0 * P:(k0 + nk) * P, COL[chunk]:COL[chunk] + cols]
                if g >= RAW_SLOTS:
                    sp.wait_ge(lo_done, g - RAW_SLOTS + 1)
                sp.dma_start(raw[:, g % RAW_SLOTS, 0:nk * cols].rearrange("p (k n) -> p k n", k=nk),
                             src.rearrange("(k p) n -> p k n", p=P)).then_inc(raw_in[g % RAW_SLOTS], 16)
            for b in range(NB):
                sp.wait_ge(x2_done, (DEPTH - 1) * 2 + b + 1)
                sp.dma_start(out[0, b * P:(b + 1) * P, :], resid[:, b, :]).then_inc(stored, 16)
            sp.wait_ge(stored, 32)

        @block.gpsimd
        def _(pool):
            chain = [0]

            def link(ins):
                chain[0] += 1
                ins.then_inc(pool_chain, 1)
                pool.wait_ge(pool_chain, chain[0])

            def bcast(vec):
                return vec.partition_broadcast(P)

            def load_p(L):
                for b in range(NB):
                    pool.dma_start(p_raw[:, b, :], p[L, 0, b * P:(b + 1) * P, :]).then_inc(p_in, 16)

            def load_small(L):
                for i, v in enumerate((lambda_q1, lambda_q2, lambda_k1, lambda_k2)):
                    pool.dma_start(lam_in[:, i, :], bcast(v[L, :])).then_inc(small_in, 16)
                pool.dma_start(g_sub[:, :], bcast(subln_g[L, :])).then_inc(small_in, 16)

            load_p(0)
            pool.dma_start(g_pre[:, :], bcast(pre_norm_g[0, :])).then_inc(gpre_in, 16)
            for b in range(NB):
                for half in range(2):
                    cols = slice(half * ROT // 2, (half + 1) * ROT // 2)
                    rows = slice(b * P, (b + 1) * P)
                    pool.dma_start(cos2[:, b, cols], rope[0, rows, :]).then_inc(rope_in, 16)
                    pool.dma_start(sin2[:, b, cols], rope[1 + half, rows, :]).then_inc(rope_in, 16)
            link(nc.gpsimd.memset(ident[:, :], 0.0))
            link(nc.gpsimd.affine_select(out=ident[:, :], in_=ident[:, :], compare_op=ALU.not_equal, fill=1.0, base=0,
                                         pattern=[[-1, P]], channel_multiplier=1))
            nc.gpsimd.tensor_copy(ident16[:, :], ident[:, :]).then_inc(const_done, 1)
            link(nc.gpsimd.memset(causal[:, :], 0.0))
            nc.gpsimd.memset(causal[0:CHUNK, SEQ - CHUNK:SEQ], NEG).then_inc(const_done, 1)
            link(nc.gpsimd.memset(minus_half[:, :], -0.5))
            load_small(0)
            pool.dma_start(g_post[:, :], bcast(post_norm_g[0, :])).then_inc(gpost_in, 16)
            pool.dma_start(g_ple[:, :], bcast(ple_norm_g[0, :])).then_inc(gple_in, 16)
            pool.wait_ge(rope_in, 16 * 8)

            rot_user = [None]

            def rope_rows(view, heads, b, done, value):
                if rot_user[0]:
                    pool.wait_ge(*rot_user[0])
                rot_user[0] = (done, value)
                lo_half, hi_half = view[:, :, 0:ROT // 2], view[:, :, ROT // 2:ROT]

                def table(t, cols):
                    return t[:, b:b + 1, cols].to_broadcast([P, heads, cols.stop - cols.start])

                nc.gpsimd.tensor_tensor(rot_a[:, 0:heads, :], view[:, :, 0:ROT], table(cos2, slice(0, ROT)), ALU.mult)
                nc.gpsimd.tensor_tensor(rot_b[:, 0:heads, 0:ROT // 2], hi_half, table(sin2, slice(0, ROT // 2)),
                                        ALU.mult)
                link(nc.gpsimd.tensor_tensor(rot_b[:, 0:heads, ROT // 2:ROT], lo_half,
                                             table(sin2, slice(ROT // 2, ROT)), ALU.mult))
                nc.gpsimd.tensor_tensor(view[:, :, 0:ROT], rot_a[:, 0:heads, :], rot_b[:, 0:heads, :],
                                        ALU.add).then_inc(done, 1)

            def inv_sqrt(i, L, b):
                pool.wait_ge(var_done[i], L * 2 + b + 1)
                nc.gpsimd.tensor_tensor(rstd[:, i, b:b + 1], var[:, i, b:b + 1], minus_half[:, 0:1],
                                        ALU.pow).then_inc(rstd_done[i], 1)

            for pos, (L, s) in enumerate(STEPS):
                kind = s[0]
                if kind == "mm":
                    chunk, n, k0, nk, cols = UNITS[s[1]]
                    b = s[2]
                    if s[1] != LAST_OF[chunk, n]:
                        continue
                    if chunk == "IDX":
                        pool.wait_ge(idx_out, L * 2 + b + 1)
                        rope_rows(z_idx[:, b, :].rearrange("p (h d) -> p h d", d=HEAD), 6, b, rope_idx,
                                  L * 2 + b + 1)
                    elif chunk in Z_ORDER:
                        pool.wait_ge(z_out, L * 8 + Z_ORDER.index(chunk) * 2 + b + 1)
                        rope_rows(z_view(chunk, b).rearrange("p (h d) -> p h d", d=HEAD), 8, b, rope_z,
                                  L * 8 + Z_ORDER.index(chunk) * 2 + b + 1)
                elif kind == "PV":
                    for gi, (g, b, members) in enumerate(PV_GROUP):
                        if g == 0 and s[1] == members[-1]:
                            pool.wait_ge(varh_done, L * 2 + b + 1)
                            nc.gpsimd.tensor_tensor(rstd_h[:, b, :], var_h[:, b, :], minus_half[:, :],
                                                    ALU.pow).then_inc(rstdh_done, 1)
                elif kind == "pre":
                    inv_sqrt(0, s[2] if len(s) > 2 else L, s[1])
                elif kind == "post0":
                    inv_sqrt(1, L, s[1])
                elif kind == "ple0":
                    inv_sqrt(2, s[2], s[1])
                elif kind == "pT":
                    nxt = 1 if pos == 0 else L + 2
                    if nxt < DEPTH:
                        pool.wait_ge(ptr_done, nxt)
                        load_p(nxt)
                if kind == "t8" and s[1] == "h" and s[2:] == (1, 1) and L + 1 < DEPTH:
                    pool.wait_ge(h_done, L * 2 + 2)
                    pool.dma_start(g_pre[:, :], bcast(pre_norm_g[L + 1, :])).then_inc(gpre_in, 16)
                if kind == "post1" and s[1] == 1 and L + 1 < DEPTH:
                    pool.wait_ge(x1_done, L * 2 + 2)
                    pool.dma_start(g_post[:, :], bcast(post_norm_g[L + 1, :])).then_inc(gpost_in, 16)
                    load_small(L + 1)
                if kind == "ple1" and s[1] == 1 and s[2] + 1 < DEPTH:
                    pool.wait_ge(x2_done, s[2] * 2 + 2)
                    pool.dma_start(g_ple[:, :], bcast(ple_norm_g[s[2] + 1, :])).then_inc(gple_in, 16)

        @block.scalar
        def _(act):
            def copy(dst, src, scale=1.0):
                return nc.scalar.activation(dst, src, ACT.Copy, scale=scale)

            junk_user = [None]

            def junk_free(sem_, value):
                if junk_user[0]:
                    act.wait_ge(*junk_user[0])
                junk_user[0] = (sem_, value)

            def square_resid(L, b):
                junk_free(sq_done[0], L * 2 + b + 1)
                nc.scalar.activation(junk[:, :], resid[:, b, :], ACT.Square, scale=D_MODEL ** -0.5,
                                     accum_out=ssq[:, 0, b, 0:1]).then_inc(sq_done[0], 1)

            for pos, (L, s) in enumerate(STEPS):
                for g in SPLITS[pos]:
                    nk, cols = UNITS[g % U][3:]
                    act.wait_ge(raw_in[g % RAW_SLOTS], 16 * (g // RAW_SLOTS + 1))
                    if g >= SLOTS:
                        act.wait_ge(unit_used, g - SLOTS + 1)
                    copy(w_hi[:, g % SLOTS, 0:nk * cols], raw[:, g % RAW_SLOTS, 0:nk * cols]).then_inc(hi_done, 1)
                kind = s[0]
                if kind == "mm":
                    chunk, n, k0, nk, cols = UNITS[s[1]]
                    b = s[2]
                    if s[1] != LAST_OF[chunk, n] or chunk in ("WO", "WG"):
                        continue
                    ps = proj[bank_of(chunk, n, b)]
                    wait_sum(act, L, chunk, n, b)
                    if chunk == "PLE":
                        if L > 0:
                            act.wait_ge(e_done, (L - 1) * 2 + b + 1)
                        copy(emb[:, b, n * N:(n + 1) * N], ps[:, :]).then_inc(ple_out, 1)
                    elif chunk == "IDX":
                        nqk = 5 * HEAD
                        copy(z_idx[:, b, 0:nqk], ps[:, 0:nqk])
                        copy(z_idx[:, b, nqk:nqk + HEAD], ps[:, 4 * HEAD:nqk])
                        copy(w_idx[:, b, :], ps[:, nqk:nqk + IDX_HEADS], IDX_HEADS ** -0.5).then_inc(idx_out, 1)
                    elif chunk in Z_ORDER:
                        copy(z_view(chunk, b), ps[:, :]).then_inc(z_out, 1)
                    elif chunk in ("VB", "VA"):
                        copy(v_all[:, b, int(chunk == "VA"), :], ps[:, :]).then_inc(v_out, 1)
                    else:
                        if chunk == "GB":
                            act.wait_ge(y_done, L * 4 + b + 1)
                        else:
                            if L > 0:
                                act.wait_ge(y_done, (L - 1) * 4 + 2 + b + 1)
                        nc.scalar.activation(gate[:, b, :], ps[:, :], ACT.Sigmoid).then_inc(sig_done, 1)
                elif kind == "pT":
                    m = 0 if pos == 0 else L + 1
                    act.wait_ge(ptr_done, m + 1)
                    copy(p_hi[:, :, :, :].rearrange("p b k t -> p (b k t)"), pv[:, :]).then_inc(p_hi_done, 1)
                elif kind == "pre":
                    b, M = s[1], (s[2] if len(s) > 2 else L)
                    if M == 0:
                        act.wait_ge(x_in[b], 16)
                    else:
                        act.wait_ge(x2_done, (M - 1) * 2 + b + 1)
                    square_resid(M, b)
                elif kind == "t8":
                    i = t8_index(s[1], s[2], s[3])
                    act.wait_ge(t8_done, L * 12 + i + 1)
                    copy(act_hi[:, s[2], 4 * s[3]:4 * s[3] + 4, :].rearrange("p k t -> p (k t)"),
                         sc[s[3]][:, :]).then_inc(at_hi, 1)
                elif kind == "TI":
                    b = s[1]
                    act.wait_ge(tr_done, tr_index(L, s))
                    copy(idxT[:, :, b * P:(b + 1) * P], tr[:, 0:3 * P].rearrange("p (j t) -> p j t", j=3))\
                        .then_inc(tr_out, 1)
                elif kind == "T":
                    chunk, b = s[1:]
                    act.wait_ge(tr_done, tr_index(L, s))
                    dst = (qT if chunk[0] == "Q" else kT)[int(chunk[1] == "A")]
                    copy(dst[:, :, b * P:(b + 1) * P], tr[:, :].rearrange("p (j t) -> p j t", j=4),
                         HEAD ** -0.5 if chunk[0] == "Q" else 1.0).then_inc(tr_out, 1)
                elif kind == "D":
                    i = s[1]
                    act.wait_ge(dots_done, L * 4 + i + 1)
                    w = 2 * P * (i // 2 + 1)
                    nc.scalar.activation(probs[:, i, 0:w], sc[i % 2][:, 0:w], ACT.Relu, scale=HEAD ** -0.5)\
                        .then_inc(relu_done, 1)
                elif kind == "S":
                    i = s[1]
                    g, b, maps, keys = s_task(i)
                    act.wait_ge(max_done, L * 12 + i + 1)
                    if i < 4:
                        act.wait_ge(score_done, L * 2 + i // 2 + 1)
                    elif i - 4 in PT_OF_S:
                        act.wait_ge(tr_done, tr_index(L, ("PT", PT_OF_S[i - 4])))
                    else:
                        act.wait_ge(mix_done, L * 3 + (i - 4) // 2 + 1)
                    for j, m in enumerate(maps):
                        last = nc.scalar.activation(probs[:, i % 4, j * keys:(j + 1) * keys],
                                                    sc[i % 2][:, j * keys:(j + 1) * keys], ACT.Exp,
                                                    bias=neg_max[:, i % 2, j:j + 1],
                                                    accum_out=row_sum[:, g, b, m:m + 1])
                    last.then_inc(exp_done, 1)
                elif kind == "PT":
                    n = s[1]
                    act.wait_ge(tr_done, tr_index(L, s))
                    if n >= 3:
                        act.wait_ge(pv_done, L * 9 + n - 2)
                    copy(pT[:, n % 3, :, :].rearrange("p t q -> p (t q)"), tr[:, :]).then_inc(tr_out, 1)
                elif kind == "PV":
                    for g, b, members in PV_GROUP:
                        if g == 0 and s[1] == members[-1]:
                            act.wait_ge(pv_done, L * 9 + members[-1] + 1)
                            act.wait_ge(mix_done, L * 3 + (1 if b == 0 else 3))
                            junk_free(sqh_done, L * 2 + b + 1)
                            for h in range(B_HEADS):
                                last = nc.scalar.activation(junk[:, h * P:(h + 1) * P], pv[:, h * P:(h + 1) * P],
                                                            ACT.Square, scale=row_rec[:, 0, b, 2 * h:2 * h + 1],
                                                            accum_out=ssq_h[:, b, h:h + 1])
                            last.then_inc(sqh_done, 1)
                elif kind == "post0":
                    b = s[1]
                    junk_free(sq_done[1], L * 2 + b + 1)
                    for n in range(2):
                        wait_sum(act, L, "WO", n, b)
                        last = nc.scalar.activation(junk[:, n * N:(n + 1) * N], proj[bank_of("WO", n, b)][:, :],
                                                    ACT.Square, scale=D_MODEL ** -0.5, accum_out=ssq[:, 1, b, n:n + 1])
                    last.then_inc(sq_done[1], 1)
                elif kind == "ple0":
                    b, M = s[1:]
                    for n in range(2):
                        wait_sum(act, M, "WG", n, b)
                        nc.scalar.activation(work[:, b, n * N:(n + 1) * N], proj[bank_of("WG", n, b)][:, :],
                                             ACT.Sigmoid).then_inc(wg_sig, 1)
                    act.wait_ge(e_done, M * 2 + b + 1)
                    junk_free(sq_done[2], M * 2 + b + 1)
                    nc.scalar.activation(junk[:, :], work[:, b, :], ACT.Square, scale=D_MODEL ** -0.5,
                                         accum_out=ssq[:, 2, b, 0:1]).then_inc(sq_done[2], 1)
                if kind == "t8" and s[1] == "h" and s[2:] == (0, 1):
                    act.wait_ge(lam_sum, L + 1)
                    nc.scalar.activation(lam_e[:, :], lam_s[:, :], ACT.Exp).then_inc(lam_exp, 1)

        @block.vector
        def _(dve):
            chain = [0]

            def link(ins):
                chain[0] += 1
                ins.then_inc(dve_chain, 1)
                dve.wait_ge(dve_chain, chain[0])

            def lambda_of(L):
                lam_init = 0.8 - 0.6 * math.exp(-0.3 * L)
                dve.wait_ge(small_in, 16 * 5 * (L + 1))
                link(nc.vector.tensor_tensor(lam_prod[:, :, :], lam_in[:, 0:2, :], lam_in[:, 2:4, :], ALU.mult))
                nc.vector.tensor_reduce(lam_s[:, :], lam_prod[:, :, :], AX.X, ALU.add).then_inc(lam_sum, 1)
                nc.vector.tensor_scalar(g_subs[:, :], g_sub[:, :], 1.0 - lam_init, None, ALU.mult)
                dve.wait_ge(lam_exp, L + 1)
                nc.vector.tensor_scalar(neg_lam[:, :], lam_e[:, 1:2], lam_e[:, 0:1], -lam_init, ALU.subtract, ALU.add)\
                    .then_inc(lam_done, 1)

            def add_eps(i, L, b, parts):
                dve.wait_ge(sq_done[i], L * 2 + b + 1)
                if parts == 2:
                    nc.vector.tensor_scalar(var[:, i, b:b + 1], ssq[:, i, b, 0:1], ssq[:, i, b, 1:2], EPS, ALU.add,
                                            ALU.add).then_inc(var_done[i], 1)
                else:
                    nc.vector.tensor_scalar(var[:, i, b:b + 1], ssq[:, i, b, 0:1], EPS, None, ALU.add)\
                        .then_inc(var_done[i], 1)

            for pos, (L, s) in enumerate(STEPS):
                for g in SPLITS[pos]:
                    nk, cols = UNITS[g % U][3:]
                    dve.wait_ge(hi_done, g + 1)
                    nc.vector.tensor_tensor(w_lo[:, g % SLOTS, 0:nk * cols], raw[:, g % RAW_SLOTS, 0:nk * cols],
                                            w_hi[:, g % SLOTS, 0:nk * cols].bitcast(fp32), ALU.subtract)\
                        .then_inc(lo_done, 1)
                kind = s[0]
                if kind == "mm":
                    chunk, n, k0, nk, cols = UNITS[s[1]]
                    b = s[2]
                    if s[1] != LAST_OF[chunk, n] or chunk not in ("GA", "GB"):
                        continue
                    g = int(chunk == "GA")
                    i = L * 4 + (0 if g else 2) + b + 1
                    dve.wait_ge(sig_done, i)
                    nc.vector.tensor_tensor(gate[:, b, :], proj[bank_of(chunk, n, b)][:, :], gate[:, b, :], ALU.mult)\
                        .then_inc(glu_done, 1)
                    dve.wait_ge(glu_done, i)
                    dve.wait_ge(pv_out, L * 4 + 2 * g + b + 1)
                    nc.vector.tensor_tensor(y_mix[g][:, b, :], y_mix[g][:, b, :], gate[:, b, :], ALU.mult)\
                        .then_inc(y_done, 1)
                elif kind == "pT":
                    m = 0 if pos == 0 else L + 1
                    dve.wait_ge(p_hi_done, m + 1)
                    nc.vector.tensor_tensor(p_lo[:, :, :, :].rearrange("p b k t -> p (b k t)"), pv[:, :],
                                            p_hi[:, :, :, :].rearrange("p b k t -> p (b k t)").bitcast(fp32),
                                            ALU.subtract).then_inc(p_lo_done, 1)
                elif kind == "pre":
                    b, M = s[1], (s[2] if len(s) > 2 else L)
                    add_eps(0, M, b, 1)
                    dve.wait_ge(rstd_done[0], M * 2 + b + 1)
                    dve.wait_ge(gpre_in, 16 * (M + 1))
                    nc.vector.scalar_tensor_tensor(work[:, b, :], resid[:, b, :], rstd[:, 0, b:b + 1], g_pre[:, :],
                                                   ALU.mult, ALU.mult).then_inc(h_done, 1)
                elif kind == "t8":
                    i = t8_index(s[1], s[2], s[3])
                    dve.wait_ge(at_hi, L * 12 + i + 1)
                    nc.vector.tensor_tensor(act_lo[:, s[2], 4 * s[3]:4 * s[3] + 4, :].rearrange("p k t -> p (k t)"),
                                            sc[s[3]][:, :],
                                            act_hi[:, s[2], 4 * s[3]:4 * s[3] + 4, :].rearrange("p k t -> p (k t)")
                                            .bitcast(fp32), ALU.subtract).then_inc(at_lo, 1)
                    if s[1:] == ("h", 0, 1):
                        lambda_of(L)
                elif kind == "D":
                    b, odd = divmod(s[1], 2)
                    if not odd:
                        continue
                    keys = (b + 1) * P
                    dve.wait_ge(relu_done, L * 4 + s[1] + 1)
                    for h in range(IDX_HEADS):
                        r = probs[:, 2 * b + h % 2, (h // 2) * keys:(h // 2 + 1) * keys]
                        w = w_idx[:, b, h:h + 1]
                        if h == 0:
                            ins = nc.vector.tensor_scalar(score[b][:, :], r, w, None, ALU.mult)
                        else:
                            ins = nc.vector.scalar_tensor_tensor(score[b][:, :], r, w, score[b][:, :], ALU.mult,
                                                                 ALU.add)
                        if h + 1 < IDX_HEADS:
                            link(ins)
                    ins.then_inc(score_done, 1)
                elif kind == "topk":
                    b, r = s[1:]
                    keys = (b + 1) * P
                    if r == 0:
                        dve.wait_ge(score_done, L * 2 + b + 1)
                        link(nc.vector.memset(score[b][0:CHUNK, keys - CHUNK:keys], INADMISSIBLE))
                    link(nc.vector.max(top8[:, :], score[b][:, :]))
                    link(nc.vector.match_replace(score[b][:, :], top8[:, :], score[b][:, :], TAKEN))
                    if r == TOPK // 8 - 1:
                        nc.vector.tensor_scalar(sel_mask[b][:, :], score[b][:, :], TAKEN, NEG, ALU.is_gt, ALU.mult)\
                            .then_inc(mask_done, 1)
                elif kind == "S":
                    i = s[1]
                    g, b, maps, keys = s_task(i)
                    dve.wait_ge(s_done, L * 12 + i + 1)
                    if L * 12 + i >= 2:
                        dve.wait_ge(exp_done, L * 12 + i - 1)
                    nc.vector.tensor_reduce(neg_max[:, i % 2, 0:len(maps)],
                                            sc[i % 2][:, :].rearrange("p (m k) -> p m k", k=keys), AX.X, ALU.max,
                                            negate=True).then_inc(max_done, 1)
                    dve.wait_ge(exp_done, L * 12 + i + 1)
                    own = slice(maps[0], maps[-1] + 1, 2)
                    rec = nc.vector.reciprocal(row_rec[:, g, b, own], row_sum[:, g, b, own])
                    if g == 0 and i % 2:
                        link(rec)
                        if L * 3 + i // 2:
                            dve.wait_ge(mix_done, L * 3 + i // 2)
                        for j, m in enumerate(maps):
                            ins = nc.vector.scalar_tensor_tensor(mix_c[:, j:j + 1], row_rec[:, 0, b, m:m + 1],
                                                                 neg_lam[:, :], row_sum[:, 0, b, m - 1:m], ALU.mult,
                                                                 ALU.mult)
                        link(ins)
                        for j in range(len(maps)):
                            p1 = probs[:, (i - 1) % 4, j * keys:(j + 1) * keys]
                            p2 = probs[:, i % 4, j * keys:(j + 1) * keys]
                            ins = nc.vector.scalar_tensor_tensor(p1, p2, mix_c[:, j:j + 1], p1, ALU.mult, ALU.add)
                        ins.then_inc(mix_done, 1)
                elif kind == "PV":
                    for gi, (g, b, members) in enumerate(PV_GROUP):
                        if s[1] != members[-1]:
                            continue
                        if g == 1:
                            dve.wait_ge(pv_done, L * 9 + members[-1] + 1)
                            nc.vector.tensor_tensor(
                                y_mix[1][:, b, :].rearrange("p (h d) -> p h d", d=HEAD),
                                pv[:, :].rearrange("p (h d) -> p h d", d=HEAD),
                                row_rec[:, 1, b, :].unsqueeze(2).to_broadcast([P, 8, HEAD]), ALU.mult)\
                                .then_inc(pv_out, 1)
                        else:
                            dve.wait_ge(sqh_done, L * 2 + b + 1)
                            nc.vector.tensor_scalar(var_h[:, b, :], ssq_h[:, b, :], 1.0 / P, EPS, ALU.mult, ALU.add)\
                                .then_inc(varh_done, 1)
                            dve.wait_ge(rstdh_done, L * 2 + b + 1)
                            link(nc.vector.tensor_tensor(scale_h[:, b, :], rstd_h[:, b, :],
                                                         row_rec[:, 0, b, :].rearrange("p (h c) -> p h c", c=2)[:, :, 0],
                                                         ALU.mult))
                            for h in range(B_HEADS):
                                ins = nc.vector.scalar_tensor_tensor(
                                    y_mix[0][:, b, h * P:(h + 1) * P], pv[:, h * P:(h + 1) * P],
                                    scale_h[:, b, h:h + 1], g_subs[:, :], ALU.mult, ALU.mult)
                            ins.then_inc(pv_out, 1)
                elif kind == "post0":
                    add_eps(1, L, s[1], 2)
                elif kind == "post1":
                    b = s[1]
                    dve.wait_ge(rstd_done[1], L * 2 + b + 1)
                    dve.wait_ge(gpost_in, 16 * (L + 1))
                    for n in range(2):
                        nc.vector.scalar_tensor_tensor(work[:, b, n * N:(n + 1) * N],
                                                       proj[bank_of("WO", n, b)][:, :], rstd[:, 1, b:b + 1],
                                                       g_post[:, n * N:(n + 1) * N], ALU.mult, ALU.mult)\
                            .then_inc(wo_scaled, 1)
                    dve.wait_ge(wo_scaled, L * 4 + 2 * b + 2)
                    nc.vector.tensor_tensor(resid[:, b, :], resid[:, b, :], work[:, b, :], ALU.add)\
                        .then_inc(x1_done, 1)
                elif kind == "ple0":
                    b, M = s[1:]
                    dve.wait_ge(wg_sig, M * 4 + 2 * b + 2)
                    nc.vector.tensor_tensor(work[:, b, :], work[:, b, :], emb[:, b, :], ALU.mult).then_inc(e_done, 1)
                    add_eps(2, M, b, 1)
                elif kind == "ple1":
                    b, M = s[1:]
                    dve.wait_ge(rstd_done[2], M * 2 + b + 1)
                    dve.wait_ge(gple_in, 16 * (M + 1))
                    link(nc.vector.scalar_tensor_tensor(work[:, b, :], work[:, b, :], rstd[:, 2, b:b + 1], g_ple[:, :],
                                                        ALU.mult, ALU.mult))
                    nc.vector.tensor_tensor(resid[:, b, :], resid[:, b, :], work[:, b, :], ALU.add)\
                        .then_inc(x2_done, 1)

        @block.tensor
        def _(pe):
            def wait_bank(L, chunk, n, b):
                prev = L - 1
                if chunk == "PLE":
                    if L > 0:
                        pe.wait_ge(wg_sig, prev * 4 + (1 if n == 0 else 3) + b)
                elif chunk == "IDX":
                    pe.wait_ge(ple_out, L * 4 + 2 + b + 1)
                elif chunk == "QB":
                    pe.wait_ge(ple_out, L * 4 + b + 1)
                elif chunk == "KB":
                    pe.wait_ge(idx_out, L * 2 + b + 1)
                elif chunk == "VB":
                    pe.wait_ge(z_out, L * 8 + b + 1)
                elif chunk == "QA":
                    pe.wait_ge(z_out, L * 8 + 2 + b + 1)
                elif chunk == "KA":
                    pe.wait_ge(v_out, L * 4 + b + 1)
                elif chunk == "VA":
                    pe.wait_ge(z_out, L * 8 + 4 + b + 1)
                elif chunk == "GA":
                    pe.wait_ge(z_out, L * 8 + 6 + b + 1)
                elif chunk == "GB":
                    pe.wait_ge(v_out, L * 4 + 2 + b + 1)
                elif chunk == "WO":
                    pe.wait_ge(glu_done, L * 4 + 2 * b + n + 1)
                else:
                    pe.wait_ge(wo_scaled, L * 4 + 2 * b + n + 1)

            def wait_tr(L, s):
                i = tr_index(L, s)
                if i > 1:
                    pe.wait_ge(tr_out, i - 1)

            pe.wait_ge(const_done, 2)
            for pos, (L, s) in enumerate(STEPS):
                kind = s[0]
                if kind == "mm":
                    u, b = s[1:]
                    g = L * U + u
                    chunk, n, k0, nk, cols = UNITS[u]
                    ps = proj[bank_of(chunk, n, b)][:, 0:cols]
                    if k0 == 0:
                        wait_bank(L, chunk, n, b)
                    pe.wait_ge(lo_done, g + 1)
                    if chunk == "PLE":
                        pe.wait_ge(p_lo_done, L + 1)
                        src_hi, src_lo = p_hi, p_lo
                    else:
                        src = "y" if chunk == "WO" else "x" if chunk == "WG" else "h"
                        pe.wait_ge(at_lo, L * 12 + t8_index(src, b, k0 // 4) + 1)
                        src_hi, src_lo = act_hi, act_lo
                    for k in range(nk):
                        hi = w_hi[:, g % SLOTS, k * cols:(k + 1) * cols]
                        lo = w_lo[:, g % SLOTS, k * cols:(k + 1) * cols]
                        last_k = u == LAST_OF[chunk, n] and k == nk - 1
                        nc.tensor.matmul(ps, src_hi[:, b, k0 + k, :], hi, start=(k0 + k == 0), stop=False)
                        nc.tensor.matmul(ps, src_hi[:, b, k0 + k, :], lo, start=False, stop=False)
                        last = nc.tensor.matmul(ps, src_lo[:, b, k0 + k, :], hi, start=False, stop=last_k)
                    if b == 1:
                        last.then_inc(unit_used, 1)
                    elif last_k:
                        last.then_inc(b0_done, 1)
                elif kind == "pT":
                    m = 0 if pos == 0 else L + 1
                    pe.wait_ge(p_in, 32 * (m + 1))
                    if m > 0:
                        pe.wait_ge(pv_out, m * 4)
                    for b in range(NB):
                        for k in range(D_PLE // P):
                            j = b * 2 + k
                            last = nc.tensor.transpose(pv[:, j * P:(j + 1) * P], p_raw[:, b, k * P:(k + 1) * P],
                                                       ident[:, :])
                    last.then_inc(ptr_done, 1)
                elif kind == "t8":
                    src, b, half = s[1:]
                    i = t8_index(src, b, half)
                    if src == "h":
                        pe.wait_ge(h_done, L * 2 + b + 1)
                    elif src == "y":
                        pe.wait_ge(y_done, L * 4 + 2 + b + 1)
                    else:
                        pe.wait_ge(x1_done, L * 2 + b + 1)
                    if i in (4, 5):
                        pe.wait_ge(exp_done, L * 12 + 7 + i)
                    elif L * 12 + i >= 2:
                        pe.wait_ge(at_lo, L * 12 + i - 1)
                    for j in range(4):
                        k = 4 * half + j
                        if src == "h":
                            tile = work[:, b, k * P:(k + 1) * P]
                        elif src == "y":
                            tile = y_mix[1 - half][:, b, j * P:(j + 1) * P]
                        else:
                            tile = resid[:, b, k * P:(k + 1) * P]
                        last = nc.tensor.transpose(sc[half][:, j * P:(j + 1) * P], tile, ident[:, :])
                    last.then_inc(t8_done, 1)
                elif kind == "TI":
                    b = s[1]
                    wait_tr(L, s)
                    pe.wait_ge(rope_idx, L * 2 + b + 1)
                    for j in range(3):
                        last = nc.tensor.transpose(tr[:, j * P:(j + 1) * P], z_idx[:, b, j * P:(j + 1) * P],
                                                   ident[:, :])
                    last.then_inc(tr_done, 1)
                elif kind == "T":
                    chunk, b = s[1:]
                    wait_tr(L, s)
                    pe.wait_ge(rope_z, L * 8 + Z_ORDER.index(chunk) * 2 + b + 1)
                    z = z_view(chunk, b)
                    for j in range(4):
                        last = nc.tensor.transpose(tr[:, j * P:(j + 1) * P], z[:, j * P:(j + 1) * P], ident[:, :])
                    last.then_inc(tr_done, 1)
                elif kind == "D":
                    i = s[1]
                    b, odd = divmod(i, 2)
                    keys = (b + 1) * P
                    pe.wait_ge(tr_out, tr_index(L, ("TI", b)))
                    if i < 2:
                        pe.wait_ge(at_lo, L * 12 + 3 + i)
                    else:
                        pe.wait_ge(relu_done, L * 4 + i - 1)
                    rows = slice(odd * HEAD, (odd + 1) * HEAD)
                    for j in range(2):
                        last = nc.tensor.matmul(sc[i % 2][:, j * keys:(j + 1) * keys],
                                                idxT[rows, j, b * P:(b + 1) * P], idxT[rows, 2, 0:keys],
                                                start=True, stop=True)
                    last.then_inc(dots_done, 1)
                elif kind == "S":
                    i = s[1]
                    g, b, maps, keys = s_task(i)
                    pe.wait_ge(tr_out, tr_index(L, ("T", "KB" if g == 0 else "KA", b)))
                    if i < 2:
                        pe.wait_ge(relu_done, L * 4 + 3 + i)
                    else:
                        pe.wait_ge(exp_done, L * 12 + i - 1)
                    if g == 1:
                        pe.wait_ge(mask_done, L * 2 + b + 1)
                        mask = sel_mask[b][:, :]
                    else:
                        mask = causal[:, SEQ - keys:SEQ]
                    for j, m in enumerate(maps):
                        rows = slice((m % 2) * HEAD, (m % 2 + 1) * HEAD)
                        ps = sc[i % 2][:, j * keys:(j + 1) * keys]
                        nc.tensor.matmul(ps, qT[g][rows, m // 2, b * P:(b + 1) * P], kT[g][rows, m // 2, 0:keys],
                                         start=True, stop=False)
                        last = nc.tensor.matmul(ps, ident16[:, :], mask, start=False, stop=True)
                    last.then_inc(s_done, 1)
                elif kind == "PT":
                    n = s[1]
                    g, b, tiles = pt_task(n)
                    wait_tr(L, s)
                    if g == 0:
                        pe.wait_ge(mix_done, L * 3 + n + 1)
                    else:
                        pe.wait_ge(exp_done, L * 12 + tiles[0][2] + 1)
                    for j, (h, kt, si, col) in enumerate(tiles):
                        last = nc.tensor.transpose(tr[:, j * P:(j + 1) * P], probs[:, si % 4, col:col + P],
                                                   ident[:, :])
                    last.then_inc(tr_done, 1)
                elif kind == "PV":
                    n = s[1]
                    g, b, tiles = pt_task(n)
                    width = P if g == 0 else HEAD
                    pe.wait_ge(tr_out, tr_index(L, ("PT", n)))
                    pe.wait_ge(v_out, L * 4 + 2 * g + b + 1)
                    if n == 0:
                        pe.wait_ge(p_lo_done, L + 1)
                    for gi, (_, _, members) in enumerate(PV_GROUP):
                        if gi and n == members[0]:
                            pe.wait_ge(pv_out, L * 4 + gi)
                    for j, (h, kt, si, col) in enumerate(tiles):
                        last = nc.tensor.matmul(pv[:, h * width:(h + 1) * width], pT[:, n % 3, j, :],
                                                v_all[:, kt, g, h * width:(h + 1) * width], start=(kt == 0),
                                                stop=(kt == b))
                    last.then_inc(pv_done, 1)


_INS = ["x", "p", "pre_norm_g", "w_in", "w_out", "post_norm_g", "lambda_q1", "lambda_k1", "lambda_q2", "lambda_k2",
        "subln_g", "w_ple_gate", "w_ple_proj", "ple_norm_g"]


def kernel(**inputs):
    import numpy as _np
    import concourse.bacc as _bacc
    from concourse import mybir as _mybir
    from concourse.bass_utils import run_bass_kernel_spmd as _run

    nc = _bacc.Bacc("TRN2", target_bir_lowering=False, num_devices=1)
    arrays, args = {}, []
    for name in _INS:
        a = _np.ascontiguousarray(inputs[name])
        arrays[f"in_{name}_dram"] = a
        args.append(nc.dram_tensor(f"in_{name}_dram", a.shape, _mybir.dt.from_np(a.dtype), kind="ExternalInput").ap())
    f32 = _np.float32
    inv = f32(500000.0) ** (-_np.arange(0, ROT, 2, dtype=f32) / f32(ROT))
    angle = _np.arange(SEQ, dtype=f32)[:, None] * inv[None, :]
    table = _np.stack([_np.cos(angle), -_np.sin(angle), _np.sin(angle)]).astype(f32)
    arrays["rope_dram"] = table
    args.append(nc.dram_tensor("rope_dram", table.shape, _mybir.dt.float32, kind="ExternalInput").ap())
    args.append(nc.dram_tensor("out_0_dram", (1, SEQ, D_MODEL), _mybir.dt.float32, kind="ExternalOutput").ap())
    build(nc, *args)
    r = _run(nc, [arrays], core_ids=[0])
    return r.results[0]["out_0_dram"]
```

```python
import math
from contextlib import ExitStack

import concourse.bass as bass
from concourse import mybir

DEPTH, SEQ, D_MODEL, D_PLE = 2, 256, 1024, 256
P = 128
NB = SEQ // P
KT = D_MODEL // P
HEAD = 64
CHUNK = 64
TOPK = min(256, SEQ // 4)
D_HALF = D_MODEL // 2
A_HEADS, B_HEADS, IDX_HEADS = 8, 4, 4
ROT = HEAD // 4
EPS = 1e-6
NEG = -1e30
INADMISSIBLE = -1e38
TAKEN = -3e38
IDX_W = IDX_HEADS * HEAD + HEAD + IDX_HEADS
N = 512

_sizes = [D_HALF, D_HALF, D_HALF, IDX_HEADS * HEAD, HEAD, IDX_HEADS, D_HALF, D_HALF, D_HALF, D_HALF, D_HALF]
_off = [sum(_sizes[:i]) for i in range(len(_sizes))]
COL = dict(QA=_off[0], KA=_off[1], VA=_off[2], IDX=_off[3], GA=_off[6], QB=_off[7], KB=_off[8], VB=_off[9],
           GB=_off[10])

KU = 2
IN_CHUNKS = ["IDX", "QB", "KB", "VB", "QA", "KA", "VA", "GA", "GB"]
UNITS = [("PLE", n, 0, KU, N) for n in range(2)]
for _c in IN_CHUNKS:
    UNITS += [(_c, 0, k, KU, IDX_W if _c == "IDX" else N) for k in range(0, KT, KU)]
for _c in ("WO", "WG"):
    UNITS += [(_c, n, k, KU, N) for n in range(2) for k in range(0, KT, KU)]
U = len(UNITS)
FIRST = {}
for _i, _u in enumerate(UNITS):
    FIRST.setdefault(_u[0], _i)
LAST_OF = {(_u[0], _u[1]): _i for _i, _u in enumerate(UNITS)}
UQ = KT // KU
B0_ORDER = [("PLE", 0), ("PLE", 1)] + [(c, 0) for c in IN_CHUNKS] + [("WO", 0), ("WO", 1), ("WG", 0), ("WG", 1)]
RAW_SLOTS, SLOTS = 5, 11
START = [1, 2, 5, 6, 7, 11, 12, 13, 15, 17, 19]
UE = KU * N


def layer_steps(L):
    out = []

    def mms(chunk, order, side):
        for i, (u, b) in enumerate(order):
            out.append(("mm", FIRST[chunk] + u, b))
            out.extend(side.get(i, ()))

    both = [(u, b) for u in range(UQ) for b in range(NB)]
    one = lambda b, n=UQ: [(u, b) for u in range(n)]
    ple = [(n, b) for n in range(2) for b in range(NB)]
    t8 = lambda src, b: [("t8", src, b, 0), ("t8", src, b, 1)]
    if L == 0:
        out += [("pT", 0), ("pre", 0, 0)]
        mms("PLE", ple, {0: [("pre", 1, 0)], 2: t8("h", 0), 3: t8("h", 1)})
        mms("IDX", both, {})
        mms("QB", both, {3: [("TI", 0)], 5: [("D", 0)], 6: [("D", 1)]})
    else:
        mms("PLE", ple, {0: [("ple0", 1, 1, L - 1)] + t8("h", 0), 2: [("ple1", 1, L - 1)]})
        mms("IDX", one(0), {0: [("pre", 1, L)]})
        mms("QB", one(0), {1: t8("h", 1)})
        mms("IDX", one(1), {})
        mms("QB", one(1), {1: [("TI", 0)], 2: [("D", 0)], 3: [("D", 1)]})
    mid = [[] for _ in range(6 * len(both))]
    placed = [(0, ("TI", 1)), (1, ("T", "QB", 0)), (2, ("D", 2)), (3, ("D", 3)), (4, ("T", "QB", 1)), (5, ("lam",)),
              (10, ("T", "KB", 0)), (12, ("T", "KB", 1)), (26, ("T", "QA", 0)), (28, ("T", "QA", 1)),
              (34, ("T", "KA", 0)), (36, ("T", "KA", 1))]
    placed += [(i, ("S", n)) for n, i in enumerate([11, 13, 15, 17, 19, 21, 35, 36, 37, 38, 40, 42])]
    placed += [(i, ("E", n)) for n, i in enumerate([11, 13, 15, 17, 19, 21, 35, 36, 37, 38, 40, 42])]
    placed += [(i, ("R", n)) for n, i in enumerate([12, 14, 16, 18, 20, 22, 37, 38, 39, 40, 42, 44])]
    placed += [(i, ("PT", n)) for n, i in enumerate([17, 21, 25, 37, 38, 40, 41, 42, 44])]
    placed += [(i, ("PV", n)) for n, i in enumerate([18, 23, 26, 40, 41, 42, 43, 44, 46])]
    placed += [(19, ("hv", 0)), (21, ("hn", 0)), (27, ("hv", 1)), (29, ("hn", 1))]
    placed += [(i, ("topk", 0, r)) for r, i in enumerate([1, 2, 3, 4, 5, 6, 7, 8])]
    placed += [(i, ("topk", 1, r)) for r, i in enumerate([9, 24, 25, 26, 27, 29, 31, 32])]
    rank = {"PV": 1, "PT": 2, "T": 3, "TI": 3, "D": 3, "S": 4, "E": 4.5, "hv": 5, "hn": 6, "R": 7, "topk": 8, "lam": 9}
    for i, step in sorted(placed, key=lambda q: (q[0], rank[q[1][0]], q[1][1:])):
        mid[i].append(step)
    for c, chunk in enumerate(["KB", "VB", "QA", "KA", "VA", "GA"]):
        mms(chunk, both, dict(enumerate(mid[c * len(both):(c + 1) * len(both)])))
    mms("GB", one(0), {})
    mms("GB", one(1), {2: t8("y", 0)})
    mms("WO", one(0, 2 * UQ), {4: t8("y", 1) + [("post0", 0, 0)]})
    mms("WO", one(1, 2 * UQ), {0: [("post0", 0, 1)], 1: [("post1", 0)], 4: [("post0", 1, 0)],
                               5: t8("x", 0) + ([("pT", L + 1)] if L + 1 < DEPTH else [])})
    mms("WG", one(0, 2 * UQ), {0: [("post0", 1, 1)], 1: [("post1", 1)], 4: [("ple0", 0, 0, L)], 5: t8("x", 1)})
    mms("WG", one(1, 2 * UQ), {0: [("ple0", 0, 1, L)], 1: [("ple1", 0, L)],
                               3: [("pre", 0, L + 1)] if L + 1 < DEPTH else [], 4: [("ple0", 1, 0, L)]})
    if L + 1 == DEPTH:
        out += [("ple0", 1, 1, L), ("ple1", 1, L)]
    return out


def all_steps():
    steps = [(L, s) for L in range(DEPTH) for s in layer_steps(L)]
    last_use = {}
    for pos, (L, s) in enumerate(steps):
        if s[0] == "mm":
            last_use[L * U + s[1]] = pos
    high, low = [[] for _ in steps], [[] for _ in steps]
    at = 0
    for g in range(DEPTH * U):
        at = max(at, START[g] if g < SLOTS else last_use[g - SLOTS] + 1)
        high[at].append(g)
        low[at + (g >= SLOTS)].append(g)
    return steps, high, low


def build(nc, x, p, pre_norm_g, w_in, w_out, post_norm_g, lambda_q1, lambda_k1, lambda_q2, lambda_k2, subln_g,
          w_ple_gate, w_ple_proj, ple_norm_g, rope, out):
    fp32, f32r, bf16 = mybir.dt.float32, mybir.dt.float32r, mybir.dt.bfloat16
    ALU, ACT, AX = mybir.AluOpType, mybir.ActivationFunctionType, mybir.AxisListType
    STEPS, HIGH, LOW = all_steps()

    ctx = ExitStack()
    with ctx:
        def sb(name, shape, dt=fp32):
            return ctx.enter_context(nc.sbuf_tensor(name, shape, dt))

        def sem(name):
            return ctx.enter_context(nc.semaphore(name))

        raw = sb("raw", [P, RAW_SLOTS, UE])
        w_hi = sb("w_hi", [P, SLOTS, UE], f32r)
        w_lo = sb("w_lo", [P, SLOTS, UE], f32r)
        resid = sb("resid", [P, NB, D_MODEL])
        work = sb("work", [P, NB, D_MODEL])
        act_hi = sb("act_hi", [P, NB, KT, P], f32r)
        act_lo = sb("act_lo", [P, NB, KT, P], f32r)
        p_raw = sb("p_raw", [P, NB, D_PLE])
        p_hi = sb("p_hi", [P, NB, D_PLE // P, P], f32r)
        p_lo = sb("p_lo", [P, NB, D_PLE // P, P], f32r)
        emb = sb("emb", [P, NB, D_MODEL])
        v_all = sb("v_all", [P, NB, 2, D_HALF])
        z_idx = v_all[:, :, 0, 0:6 * HEAD]
        gate = sb("gate", [P, NB, D_HALF])
        qT = [sb("qT_b", [P, 4, SEQ]), sb("qT_a", [P, 4, SEQ])]
        kT = sb("kT", [P, 4, SEQ])
        y_mix = [[qT[g][:, :, b * P:(b + 1) * P] for b in range(NB)] for g in range(2)]
        probs = sb("probs", [P, 4, N])
        pT = sb("pT", [P, 3, 4, P])
        idxT = pT[:, 0:2, :, :].rearrange("p a t q -> p (a t q)")[:, 0:3 * SEQ].rearrange("p (j t) -> p j t", j=3)
        score = [sb("score0", [P, P]), sb("score1", [P, SEQ])]
        sel_mask = [sb("sel_mask0", [P, P], bf16), sb("sel_mask1", [P, SEQ], bf16)]
        causal = sb("causal", [P, CHUNK], bf16)
        ident = sb("ident", [P, P])
        ident16 = sb("ident16", [P, P], bf16)
        g_norm = sb("g_norm", [P, D_MODEL])
        g_ple = sb("g_ple", [P, D_MODEL])
        g_sub = sb("g_sub", [P, P])
        lam_in = sb("lam_in", [P, 4, HEAD])
        lam_s = sb("lam_s", [P, 2])
        lam_e = sb("lam_e", [P, 2])
        neg_lam = sb("neg_lam", [P, 1])
        rot_tab = sb("rot_tab", [P, NB, 2 * ROT])
        cos2, sin2 = rot_tab[:, :, 0:ROT], rot_tab[:, :, ROT:2 * ROT]
        rot_a = sb("rot_a", [P, 8, ROT])
        rot_b = sb("rot_b", [P, 8, ROT])
        w_idx = sb("w_idx", [P, NB, IDX_HEADS])
        top8 = sb("top8", [P, 8])
        neg_max = sb("neg_max", [P, 2, 4])
        row_sum = sb("row_sum", [P, 2, NB, 8])
        row_rec = sb("row_rec", [P, 2, NB, 8])
        mix_c = sb("mix_c", [P, 4])
        ssq = sb("ssq", [P, 3, NB, 2])
        var = sb("var", [P, 3, NB])
        rstd = sb("rstd", [P, 3, NB])
        ssq_h = sb("ssq_h", [P, NB, B_HEADS])
        var_h = sb("var_h", [P, NB, B_HEADS])
        rstd_h = sb("rstd_h", [P, NB, B_HEADS])
        scale_h = sb("scale_h", [P, NB, B_HEADS])
        minus_half = sb("minus_half", [P, B_HEADS])

        proj = [ctx.enter_context(nc.psum_tensor(f"proj{i}", [P, N], fp32)) for i in range(4)]
        sc = [ctx.enter_context(nc.psum_tensor(f"sc{i}", [P, N], fp32)) for i in range(2)]
        tr = ctx.enter_context(nc.psum_tensor("tr", [P, N], fp32))
        pv = ctx.enter_context(nc.psum_tensor("pv", [P, N], fp32))

        raw_in = [sem(f"raw_in{i}") for i in range(RAW_SLOTS)]
        hi_done, lo_done = sem("hi_done"), sem("lo_done")
        unit_used = sem("unit_used")
        b0_done = sem("b0_done")
        x_in = [sem(f"x_in{b}") for b in range(NB)]
        p_in = [sem(f"p_in{L}") for L in range(DEPTH)]
        gpre_in = [sem(f"gpre_in{L}") for L in range(DEPTH)]
        rope_in, gpost_in, gple_in, small_in = (sem(n) for n in ("rope_in", "gpost_in", "gple_in", "small_in"))
        const_done = sem("const_done")
        sq_done = [sem(f"sq_done{i}") for i in range(3)]
        var_done = [sem(f"var_done{i}") for i in range(3)]
        rstd_done = [sem(f"rstd_done{i}") for i in range(3)]
        h_done, x1_done, x2_done = sem("h_done"), sem("x1_done"), sem("x2_done")
        t8_done, at_hi, at_lo = sem("t8_done"), sem("at_hi"), sem("at_lo")
        ptr_done, p_hi_done, p_lo_done = sem("ptr_done"), sem("p_hi_done"), sem("p_lo_done")
        ple_out = sem("ple_out")
        idx_out, z_out, v_out = sem("idx_out"), sem("z_out"), sem("v_out")
        rope_idx, rope_z = sem("rope_idx"), sem("rope_z")
        tr_done, tr_out = sem("tr_done"), sem("tr_out")
        dots_done, relu_done, score_done = sem("dots_done"), sem("relu_done"), sem("score_done")
        mask_done = sem("mask_done")
        s_done, max_done, exp_done, mix_done = (sem(n) for n in ("s_done", "max_done", "exp_done", "mix_done"))
        rec_done = sem("rec_done")
        pv_done, pv_out = sem("pv_done"), sem("pv_out")
        sqh_done, varh_done, rstdh_done = sem("sqh_done"), sem("varh_done"), sem("rstdh_done")
        sig_done, glu_done, y_done = sem("sig_done"), sem("glu_done"), sem("y_done")
        wo_scaled, wg_sig, e_done = sem("wo_scaled"), sem("wg_sig"), sem("e_done")
        lam_sum, lam_exp, lam_done = sem("lam_sum"), sem("lam_exp"), sem("lam_done")
        dve_chain, pool_chain = sem("dve_chain"), sem("pool_chain")
        stored = sem("stored")

        def bank_of(chunk, n, b):
            if chunk == "PLE":
                return 2 * (1 - n) + b
            if chunk in ("WO", "WG"):
                return (2 if b == 0 else 0) + n
            return 2 * (IN_CHUNKS.index(chunk) % 2) + b

        def wait_sum(eng, L, chunk, n, b):
            if b == 0:
                eng.wait_ge(b0_done, L * len(B0_ORDER) + B0_ORDER.index((chunk, n)) + 1)
            else:
                eng.wait_ge(unit_used, L * U + LAST_OF[chunk, n] + 1)

        Z_ORDER = ["QB", "KB", "QA", "KA"]

        def z_view(chunk, b):
            half = Z_ORDER.index(chunk) % 2
            return work[:, b, half * N:(half + 1) * N]

        tr_steps = [s for s in layer_steps(0) if s[0] in ("TI", "T", "PT")]
        TRN = len(tr_steps)

        def tr_index(L, s):
            return L * TRN + tr_steps.index(s) + 1

        def s_task(i):
            g, r = divmod(i, 6)
            if r < 2:
                return g, 0, list(range(r, 8, 2)), P
            q, odd = divmod(r - 2, 2)
            return g, 1, [4 * q + odd, 4 * q + odd + 2], SEQ

        def pt_task(n):
            si = [0, 2, 4, 6, 7, 8, 9, 10, 11][n]
            g, b, maps, keys = s_task(si)
            return g, b, [(m // 2 if g == 0 else m, kt, si, j * keys + kt * P)
                          for j, m in enumerate(maps) for kt in range(b + 1)]

        PT_OF_S = {}
        for n_ in range(9):
            for _, _, s_, _ in pt_task(n_)[2]:
                PT_OF_S[s_] = n_
        PV_GROUP = [(0, 0, [0]), (0, 1, [1, 2]), (1, 0, [3, 4]), (1, 1, [5, 6, 7, 8])]

        T8_BASE = dict(h=0, y=4, x=8)

        def t8_index(kind, b, half):
            return T8_BASE[kind] + 2 * b + half

        block = ctx.enter_context(nc.Block())

        @block.sync
        def _(sp):
            sp.dma_start(p_raw[:, :, :], p[0, 0].rearrange("(b p) d -> p b d", p=P)).then_inc(p_in[0], 16)
            for g in range(DEPTH * U):
                L, u = divmod(g, U)
                chunk, n, k0, nk, cols = UNITS[u]
                if chunk == "PLE":
                    src = w_ple_proj[L, :, n * N:(n + 1) * N]
                elif chunk == "WO":
                    src = w_out[L, k0 * P:(k0 + nk) * P, n * N:(n + 1) * N]
                elif chunk == "WG":
                    src = w_ple_gate[L, k0 * P:(k0 + nk) * P, n * N:(n + 1) * N]
                else:
                    src = w_in[L, k0 * P:(k0 + nk) * P, COL[chunk]:COL[chunk] + cols]
                if g >= RAW_SLOTS:
                    sp.wait_ge(lo_done, g - RAW_SLOTS + 1)
                sp.dma_start(raw[:, g % RAW_SLOTS, 0:nk * cols].rearrange("p (k n) -> p k n", k=nk),
                             src.rearrange("(k p) n -> p k n", p=P)).then_inc(raw_in[g % RAW_SLOTS], 16)
            for i in range(2 * NB):
                b, n = divmod(i, 2)
                sp.wait_ge(x2_done, (DEPTH - 1) * 4 + i + 1)
                sp.dma_start(out[0, b * P:(b + 1) * P, n * N:(n + 1) * N], resid[:, b, n * N:(n + 1) * N])\
                    .then_inc(stored, 16)
            sp.wait_ge(stored, 16 * 2 * NB)

        @block.gpsimd
        def _(pool):
            chain = [0]

            def link(ins):
                chain[0] += 1
                ins.then_inc(pool_chain, 1)
                pool.wait_ge(pool_chain, chain[0])

            def bcast(vec):
                return vec.partition_broadcast(P)

            def load_p(L):
                pool.dma_start(p_raw[:, :, :], p[L, 0].rearrange("(b p) d -> p b d", p=P)).then_inc(p_in[L], 16)

            def load_small(L):
                for i, v in enumerate((lambda_q1, lambda_q2, lambda_k1, lambda_k2)):
                    pool.dma_start(lam_in[:, i, :], bcast(v[L, :])).then_inc(small_in, 16)
                pool.dma_start(g_sub[:, :], bcast(subln_g[L, :])).then_inc(small_in, 16)

            link(nc.gpsimd.memset(ident[:, :], 0.0))
            link(nc.gpsimd.affine_select(out=ident[:, :], in_=ident[:, :], compare_op=ALU.not_equal, fill=1.0, base=0,
                                         pattern=[[-1, P]], channel_multiplier=1))
            nc.gpsimd.tensor_copy(ident16[:, :], ident[:, :]).then_inc(const_done, 1)
            link(nc.gpsimd.memset(causal[:, :], 0.0))
            nc.gpsimd.memset(causal[0:CHUNK, :], NEG).then_inc(const_done, 1)
            link(nc.gpsimd.memset(minus_half[:, :], -0.5))

            rot_user = [None]

            def rope_rows(view, heads, b, done, value):
                if rot_user[0]:
                    pool.wait_ge(*rot_user[0])
                rot_user[0] = (done, value)
                lo_half, hi_half = view[:, :, 0:ROT // 2], view[:, :, ROT // 2:ROT]

                def table(t, cols):
                    return t[:, b:b + 1, cols].to_broadcast([P, heads, cols.stop - cols.start])

                nc.gpsimd.tensor_tensor(rot_a[:, 0:heads, :], view[:, :, 0:ROT], table(cos2, slice(0, ROT)), ALU.mult)
                nc.gpsimd.tensor_tensor(rot_b[:, 0:heads, 0:ROT // 2], hi_half, table(sin2, slice(0, ROT // 2)),
                                        ALU.mult)
                link(nc.gpsimd.tensor_tensor(rot_b[:, 0:heads, ROT // 2:ROT], lo_half,
                                             table(sin2, slice(ROT // 2, ROT)), ALU.mult))
                nc.gpsimd.tensor_tensor(view[:, :, 0:ROT], rot_a[:, 0:heads, :], rot_b[:, 0:heads, :],
                                        ALU.add).then_inc(done, 1)

            def inv_sqrt(i, L, b):
                pool.wait_ge(var_done[i], L * 2 + b + 1)
                nc.gpsimd.tensor_tensor(rstd[:, i, b:b + 1], var[:, i, b:b + 1], minus_half[:, 0:1],
                                        ALU.pow).then_inc(rstd_done[i], 1)

            for pos, (L, s) in enumerate(STEPS):
                kind = s[0]
                if kind == "mm":
                    chunk, n, k0, nk, cols = UNITS[s[1]]
                    b = s[2]
                    if s[1] != LAST_OF[chunk, n]:
                        continue
                    if chunk == "IDX":
                        pool.wait_ge(rope_in, 16)
                        pool.wait_ge(idx_out, L * 2 + b + 1)
                        rope_rows(z_idx[:, b, :].rearrange("p (h d) -> p h d", d=HEAD), 6, b, rope_idx,
                                  L * 2 + b + 1)
                    elif chunk in Z_ORDER:
                        pool.wait_ge(z_out, L * 8 + Z_ORDER.index(chunk) * 2 + b + 1)
                        rope_rows(z_view(chunk, b).rearrange("p (h d) -> p h d", d=HEAD), 8, b, rope_z,
                                  L * 8 + Z_ORDER.index(chunk) * 2 + b + 1)
                elif kind == "hv":
                    b = s[1]
                    pool.wait_ge(varh_done, L * 2 + b + 1)
                    nc.gpsimd.tensor_tensor(rstd_h[:, b, :], var_h[:, b, :], minus_half[:, :], ALU.pow)\
                        .then_inc(rstdh_done, 1)
                elif kind == "pre":
                    inv_sqrt(0, s[2], s[1])
                elif kind == "post1":
                    inv_sqrt(1, L, s[1])
                elif kind == "ple1":
                    inv_sqrt(2, s[2], s[1])
                if kind == "t8" and s[1:] == ("h", 1, 1) and L + 1 < DEPTH or kind == "pT" and 0 < s[1] < DEPTH - 1:
                    m = L if kind == "t8" else s[1]
                    pool.wait_ge(ptr_done, m + 1)
                    load_p(m + 1)
                if kind == "t8" and s[1:] == ("h", 1, 1):
                    pool.wait_ge(h_done, L * 2 + 2)
                    pool.dma_start(g_norm[:, :], bcast(post_norm_g[L, :])).then_inc(gpost_in, 16)
                    if L == 0:
                        load_small(0)
                        pool.dma_start(g_ple[:, :], bcast(ple_norm_g[0, :])).then_inc(gple_in, 16)
                if kind == "post1" and s[1] == 1 and L + 1 < DEPTH:
                    pool.wait_ge(x1_done, L * 2 + 2)
                    pool.dma_start(g_norm[:, :], bcast(pre_norm_g[L + 1, :])).then_inc(gpre_in[L + 1], 16)
                    load_small(L + 1)
                if kind == "ple1" and s[1] == 1 and s[2] + 1 < DEPTH:
                    pool.wait_ge(x2_done, s[2] * 4 + 4)
                    pool.dma_start(g_ple[:, :], bcast(ple_norm_g[s[2] + 1, :])).then_inc(gple_in, 16)

        @block.scalar
        def _(act):
            def copy(dst, src, scale=1.0):
                return nc.scalar.activation(dst, src, ACT.Copy, scale=scale)

            def square_resid(L, b):
                nc.scalar.activation(work[:, b, :], resid[:, b, :], ACT.Square, scale=D_MODEL ** -0.5,
                                     accum_out=ssq[:, 0, b, 0:1]).then_inc(sq_done[0], 1)

            for b in range(NB):
                act.dma_start(resid[:, b, :], x[0, b * P:(b + 1) * P, :]).then_inc(x_in[b], 16)
                if b == 0:
                    act.dma_start(rot_tab[:, :, :], rope.rearrange("(b p) r -> p b r", p=P)).then_inc(rope_in, 16)
                    act.dma_start(g_norm[:, :], pre_norm_g[0, :].partition_broadcast(P)).then_inc(gpre_in[0], 16)
            for pos, (L, s) in enumerate(STEPS):
                for g in HIGH[pos]:
                    nk, cols = UNITS[g % U][3:]
                    act.wait_ge(raw_in[g % RAW_SLOTS], 16 * (g // RAW_SLOTS + 1))
                    if g >= SLOTS:
                        act.wait_ge(unit_used, g - SLOTS + 1)
                    copy(w_hi[:, g % SLOTS, 0:nk * cols], raw[:, g % RAW_SLOTS, 0:nk * cols]).then_inc(hi_done, 1)
                kind = s[0]
                if kind == "mm":
                    chunk, n, k0, nk, cols = UNITS[s[1]]
                    b = s[2]
                    if s[1] != LAST_OF[chunk, n] or chunk in ("WO", "WG"):
                        continue
                    ps = proj[bank_of(chunk, n, b)]
                    wait_sum(act, L, chunk, n, b)
                    if chunk == "PLE":
                        if L > 0:
                            act.wait_ge(e_done, (L - 1) * 4 + 2 * b + n + 1)
                        copy(emb[:, b, n * N:(n + 1) * N], ps[:, :]).then_inc(ple_out, 1)
                    elif chunk == "IDX":
                        nqk = 5 * HEAD
                        copy(z_idx[:, b, 0:nqk], ps[:, 0:nqk])
                        copy(z_idx[:, b, nqk:nqk + HEAD], ps[:, 4 * HEAD:nqk])
                        copy(w_idx[:, b, :], ps[:, nqk:nqk + IDX_HEADS], IDX_HEADS ** -0.5).then_inc(idx_out, 1)
                    elif chunk in Z_ORDER:
                        copy(z_view(chunk, b), ps[:, :]).then_inc(z_out, 1)
                    elif chunk in ("VB", "VA"):
                        copy(v_all[:, b, int(chunk == "VA"), :], ps[:, :]).then_inc(v_out, 1)
                    else:
                        if chunk == "GB":
                            act.wait_ge(y_done, L * 4 + b + 1)
                        else:
                            if L > 0:
                                act.wait_ge(y_done, (L - 1) * 4 + 2 + b + 1)
                        nc.scalar.activation(gate[:, b, :], ps[:, :], ACT.Sigmoid).then_inc(sig_done, 1)
                elif kind == "pT":
                    m = s[1]
                    act.wait_ge(ptr_done, m + 1)
                    copy(p_hi[:, :, :, :].rearrange("p b k t -> p (b k t)"), pv[:, :]).then_inc(p_hi_done, 1)
                elif kind == "pre":
                    b, M = s[1:]
                    if M == 0:
                        act.wait_ge(x_in[b], 16)
                    else:
                        act.wait_ge(x2_done, (M - 1) * 4 + 2 * b + 2)
                    square_resid(M, b)
                elif kind == "t8":
                    i = t8_index(s[1], s[2], s[3])
                    act.wait_ge(t8_done, L * 12 + i + 1)
                    copy(act_hi[:, s[2], 4 * s[3]:4 * s[3] + 4, :].rearrange("p k t -> p (k t)"),
                         sc[s[3]][:, :]).then_inc(at_hi, 1)
                elif kind == "TI":
                    b = s[1]
                    act.wait_ge(tr_done, tr_index(L, s))
                    copy(idxT[:, :, b * P:(b + 1) * P], tr[:, 0:3 * P].rearrange("p (j t) -> p j t", j=3))\
                        .then_inc(tr_out, 1)
                elif kind == "T":
                    chunk, b = s[1:]
                    act.wait_ge(tr_done, tr_index(L, s))
                    dst = qT[int(chunk[1] == "A")] if chunk[0] == "Q" else kT
                    copy(dst[:, :, b * P:(b + 1) * P], tr[:, :].rearrange("p (j t) -> p j t", j=4),
                         HEAD ** -0.5 if chunk[0] == "Q" else 1.0).then_inc(tr_out, 1)
                elif kind == "D":
                    i = s[1]
                    act.wait_ge(dots_done, L * 4 + i + 1)
                    w = 2 * P * (i // 2 + 1)
                    nc.scalar.activation(probs[:, i, 0:w], sc[i % 2][:, 0:w], ACT.Relu, scale=HEAD ** -0.5)\
                        .then_inc(relu_done, 1)
                elif kind == "E":
                    i = s[1]
                    g, b, maps, keys = s_task(i)
                    act.wait_ge(max_done, L * 12 + i + 1)
                    if i < 4:
                        act.wait_ge(score_done, L * 2 + i // 2 + 1)
                    elif i - 4 in PT_OF_S:
                        act.wait_ge(tr_done, tr_index(L, ("PT", PT_OF_S[i - 4])))
                    else:
                        act.wait_ge(mix_done, L * 3 + (i - 4) // 2 + 1)
                    for j, m in enumerate(maps):
                        last = nc.scalar.activation(probs[:, i % 4, j * keys:(j + 1) * keys],
                                                    sc[i % 2][:, j * keys:(j + 1) * keys], ACT.Exp,
                                                    bias=neg_max[:, i % 2, j:j + 1],
                                                    accum_out=row_sum[:, g, b, m:m + 1])
                    last.then_inc(exp_done, 1)
                elif kind == "PT":
                    n = s[1]
                    act.wait_ge(tr_done, tr_index(L, s))
                    if n >= 3:
                        act.wait_ge(pv_done, L * 9 + n - 2)
                    copy(pT[:, n % 3, :, :].rearrange("p t q -> p (t q)"), tr[:, :]).then_inc(tr_out, 1)
                elif kind == "PV":
                    for g, b, members in PV_GROUP:
                        if g == 0 and s[1] == members[-1]:
                            act.wait_ge(pv_done, L * 9 + members[-1] + 1)
                            act.wait_ge(mix_done, L * 3 + (1 if b == 0 else 3))
                            for h in range(B_HEADS):
                                last = nc.scalar.activation(y_mix[0][b][:, h, :], pv[:, h * P:(h + 1) * P],
                                                            ACT.Square, scale=row_rec[:, 0, b, 2 * h:2 * h + 1],
                                                            accum_out=ssq_h[:, b, h:h + 1])
                            last.then_inc(sqh_done, 1)
                elif kind == "post0":
                    b, n = s[1:]
                    wait_sum(act, L, "WO", n, b)
                    nc.scalar.activation(work[:, b, n * N:(n + 1) * N], proj[bank_of("WO", n, b)][:, :], ACT.Square,
                                         scale=D_MODEL ** -0.5, accum_out=ssq[:, 1, b, n:n + 1]).then_inc(sq_done[1], 1)
                elif kind == "ple0":
                    b, n, M = s[1:]
                    wait_sum(act, M, "WG", n, b)
                    half = work[:, b, n * N:(n + 1) * N]
                    nc.scalar.activation(half, proj[bank_of("WG", n, b)][:, :], ACT.Sigmoid).then_inc(wg_sig, 1)
                    act.wait_ge(e_done, M * 4 + 2 * b + n + 1)
                    if 2 * b + n:
                        act.wait_ge(sq_done[2], M * 4 + 2 * b + n)
                    nc.scalar.activation(gate[:, 1, :], half, ACT.Square, scale=D_MODEL ** -0.5,
                                         accum_out=ssq[:, 2, b, n:n + 1]).then_inc(sq_done[2], 1)
                elif kind == "lam":
                    act.wait_ge(lam_sum, L + 1)
                    nc.scalar.activation(lam_e[:, :], lam_s[:, :], ACT.Exp).then_inc(lam_exp, 1)

        @block.vector
        def _(dve):
            chain = [0]

            def link(ins):
                chain[0] += 1
                ins.then_inc(dve_chain, 1)
                dve.wait_ge(dve_chain, chain[0])

            def lambda_of(L):
                lam_init = 0.8 - 0.6 * math.exp(-0.3 * L)
                dve.wait_ge(small_in, 16 * 5 * (L + 1))
                link(nc.vector.tensor_tensor(lam_in[:, 0:2, :], lam_in[:, 0:2, :], lam_in[:, 2:4, :], ALU.mult))
                nc.vector.tensor_reduce(lam_s[:, :], lam_in[:, 0:2, :], AX.X, ALU.add).then_inc(lam_sum, 1)
                nc.vector.tensor_scalar(g_sub[:, :], g_sub[:, :], 1.0 - lam_init, None, ALU.mult)
                dve.wait_ge(lam_exp, L + 1)
                nc.vector.tensor_scalar(neg_lam[:, :], lam_e[:, 1:2], lam_e[:, 0:1], -lam_init, ALU.subtract, ALU.add)\
                    .then_inc(lam_done, 1)

            def add_eps(i, L, b, parts):
                dve.wait_ge(sq_done[i], parts * (L * 2 + b + 1))
                if parts == 2:
                    nc.vector.tensor_scalar(var[:, i, b:b + 1], ssq[:, i, b, 0:1], ssq[:, i, b, 1:2], EPS, ALU.add,
                                            ALU.add).then_inc(var_done[i], 1)
                else:
                    nc.vector.tensor_scalar(var[:, i, b:b + 1], ssq[:, i, b, 0:1], EPS, None, ALU.add)\
                        .then_inc(var_done[i], 1)

            for pos, (L, s) in enumerate(STEPS):
                for g in LOW[pos]:
                    nk, cols = UNITS[g % U][3:]
                    dve.wait_ge(hi_done, g + 1)
                    nc.vector.tensor_tensor(w_lo[:, g % SLOTS, 0:nk * cols], raw[:, g % RAW_SLOTS, 0:nk * cols],
                                            w_hi[:, g % SLOTS, 0:nk * cols].bitcast(fp32), ALU.subtract)\
                        .then_inc(lo_done, 1)
                kind = s[0]
                if kind == "mm":
                    chunk, n, k0, nk, cols = UNITS[s[1]]
                    b = s[2]
                    if s[1] != LAST_OF[chunk, n] or chunk not in ("GA", "GB"):
                        continue
                    g = int(chunk == "GA")
                    i = L * 4 + (0 if g else 2) + b + 1
                    dve.wait_ge(sig_done, i)
                    nc.vector.tensor_tensor(gate[:, b, :], proj[bank_of(chunk, n, b)][:, :], gate[:, b, :], ALU.mult)\
                        .then_inc(glu_done, 1)
                    dve.wait_ge(glu_done, i)
                    dve.wait_ge(pv_out, L * 4 + 2 * g + b + 1)
                    nc.vector.tensor_tensor(y_mix[g][b], y_mix[g][b],
                                            gate[:, b, :].rearrange("p (j t) -> p j t", j=4), ALU.mult)\
                        .then_inc(y_done, 1)
                elif kind == "pT":
                    m = s[1]
                    dve.wait_ge(p_hi_done, m + 1)
                    nc.vector.tensor_tensor(p_lo[:, :, :, :].rearrange("p b k t -> p (b k t)"), pv[:, :],
                                            p_hi[:, :, :, :].rearrange("p b k t -> p (b k t)").bitcast(fp32),
                                            ALU.subtract).then_inc(p_lo_done, 1)
                elif kind == "pre":
                    b, M = s[1:]
                    add_eps(0, M, b, 1)
                    dve.wait_ge(rstd_done[0], M * 2 + b + 1)
                    dve.wait_ge(gpre_in[M], 16)
                    nc.vector.scalar_tensor_tensor(work[:, b, :], resid[:, b, :], rstd[:, 0, b:b + 1], g_norm[:, :],
                                                   ALU.mult, ALU.mult).then_inc(h_done, 1)
                elif kind == "t8":
                    i = t8_index(s[1], s[2], s[3])
                    dve.wait_ge(at_hi, L * 12 + i + 1)
                    nc.vector.tensor_tensor(act_lo[:, s[2], 4 * s[3]:4 * s[3] + 4, :].rearrange("p k t -> p (k t)"),
                                            sc[s[3]][:, :],
                                            act_hi[:, s[2], 4 * s[3]:4 * s[3] + 4, :].rearrange("p k t -> p (k t)")
                                            .bitcast(fp32), ALU.subtract).then_inc(at_lo, 1)
                elif kind == "D":
                    b, odd = divmod(s[1], 2)
                    if not odd:
                        continue
                    keys = (b + 1) * P
                    dve.wait_ge(relu_done, L * 4 + s[1] + 1)
                    for h in range(IDX_HEADS):
                        r = probs[:, 2 * b + h % 2, (h // 2) * keys:(h // 2 + 1) * keys]
                        w = w_idx[:, b, h:h + 1]
                        if h == 0:
                            ins = nc.vector.tensor_scalar(score[b][:, :], r, w, None, ALU.mult)
                        else:
                            ins = nc.vector.scalar_tensor_tensor(score[b][:, :], r, w, score[b][:, :], ALU.mult,
                                                                 ALU.add)
                        if h + 1 < IDX_HEADS:
                            link(ins)
                    ins.then_inc(score_done, 1)
                elif kind == "topk":
                    b, r = s[1:]
                    keys = (b + 1) * P
                    if r == 0:
                        dve.wait_ge(score_done, L * 2 + b + 1)
                        link(nc.vector.memset(score[b][0:CHUNK, keys - CHUNK:keys], INADMISSIBLE))
                    link(nc.vector.max(top8[:, :], score[b][:, :]))
                    link(nc.vector.match_replace(score[b][:, :], top8[:, :], score[b][:, :], TAKEN))
                    if r == TOPK // 8 - 1:
                        nc.vector.tensor_scalar(sel_mask[b][:, :], score[b][:, :], TAKEN, NEG, ALU.is_gt, ALU.mult)\
                            .then_inc(mask_done, 1)
                elif kind == "S":
                    i = s[1]
                    g, b, maps, keys = s_task(i)
                    dve.wait_ge(s_done, L * 12 + i + 1)
                    if L * 12 + i >= 2:
                        dve.wait_ge(exp_done, L * 12 + i - 1)
                    nc.vector.tensor_reduce(neg_max[:, i % 2, 0:len(maps)],
                                            sc[i % 2][:, :].rearrange("p (m k) -> p m k", k=keys), AX.X, ALU.max,
                                            negate=True).then_inc(max_done, 1)
                elif kind == "R":
                    i = s[1]
                    g, b, maps, keys = s_task(i)
                    dve.wait_ge(exp_done, L * 12 + i + 1)
                    own = slice(maps[0], maps[-1] + 1, 2)
                    rec = nc.vector.reciprocal(row_rec[:, g, b, own], row_sum[:, g, b, own])
                    if g == 0 and i % 2:
                        link(rec)
                        if L * 3 + i // 2:
                            dve.wait_ge(mix_done, L * 3 + i // 2)
                        for j, m in enumerate(maps):
                            ins = nc.vector.scalar_tensor_tensor(mix_c[:, j:j + 1], row_rec[:, 0, b, m:m + 1],
                                                                 neg_lam[:, :], row_sum[:, 0, b, m - 1:m], ALU.mult,
                                                                 ALU.mult)
                        link(ins)
                        for j in range(len(maps)):
                            p1 = probs[:, (i - 1) % 4, j * keys:(j + 1) * keys]
                            p2 = probs[:, i % 4, j * keys:(j + 1) * keys]
                            ins = nc.vector.scalar_tensor_tensor(p1, p2, mix_c[:, j:j + 1], p1, ALU.mult, ALU.add)
                        ins.then_inc(mix_done, 1)
                    elif g == 1:
                        rec.then_inc(rec_done, 1)
                elif kind == "PV":
                    for gi, (g, b, members) in enumerate(PV_GROUP):
                        if s[1] != members[-1]:
                            continue
                        if g == 1:
                            dve.wait_ge(pv_done, L * 9 + members[-1] + 1)
                            dve.wait_ge(rec_done, L * 6 + (2 if b == 0 else 6))
                            nc.vector.tensor_tensor(
                                y_mix[1][b].rearrange("p j (h d) -> p j h d", d=HEAD),
                                pv[:, :].rearrange("p (j h d) -> p j h d", h=2, d=HEAD),
                                row_rec[:, 1, b, :].rearrange("p (j h) -> p j h", h=2).unsqueeze(3)
                                .to_broadcast([P, 4, 2, HEAD]), ALU.mult)\
                                .then_inc(pv_out, 1)
                elif kind == "hv":
                    b = s[1]
                    dve.wait_ge(sqh_done, L * 2 + b + 1)
                    nc.vector.tensor_scalar(var_h[:, b, :], ssq_h[:, b, :], 1.0 / P, EPS, ALU.mult, ALU.add)\
                        .then_inc(varh_done, 1)
                elif kind == "hn":
                    b = s[1]
                    dve.wait_ge(rstdh_done, L * 2 + b + 1)
                    link(nc.vector.tensor_tensor(scale_h[:, b, :], rstd_h[:, b, :],
                                                 row_rec[:, 0, b, :].rearrange("p (h c) -> p h c", c=2)[:, :, 0],
                                                 ALU.mult))
                    for h in range(B_HEADS):
                        ins = nc.vector.scalar_tensor_tensor(
                            y_mix[0][b][:, h, :], pv[:, h * P:(h + 1) * P],
                            scale_h[:, b, h:h + 1], g_sub[:, :], ALU.mult, ALU.mult)
                    ins.then_inc(pv_out, 1)
                elif kind == "lam":
                    lambda_of(L)
                elif kind == "post1":
                    b = s[1]
                    add_eps(1, L, b, 2)
                    dve.wait_ge(rstd_done[1], L * 2 + b + 1)
                    dve.wait_ge(gpost_in, 16 * (L + 1))
                    for n in range(2):
                        nc.vector.scalar_tensor_tensor(work[:, b, n * N:(n + 1) * N],
                                                       proj[bank_of("WO", n, b)][:, :], rstd[:, 1, b:b + 1],
                                                       g_norm[:, n * N:(n + 1) * N], ALU.mult, ALU.mult)\
                            .then_inc(wo_scaled, 1)
                    dve.wait_ge(wo_scaled, L * 4 + 2 * b + 2)
                    nc.vector.tensor_tensor(resid[:, b, :], resid[:, b, :], work[:, b, :], ALU.add)\
                        .then_inc(x1_done, 1)
                elif kind == "ple0":
                    b, n, M = s[1:]
                    half = work[:, b, n * N:(n + 1) * N]
                    dve.wait_ge(wg_sig, M * 4 + 2 * b + n + 1)
                    nc.vector.tensor_tensor(half, half, emb[:, b, n * N:(n + 1) * N], ALU.mult).then_inc(e_done, 1)
                elif kind == "ple1":
                    b, M = s[1:]
                    add_eps(2, M, b, 2)
                    dve.wait_ge(rstd_done[2], M * 2 + b + 1)
                    dve.wait_ge(gple_in, 16 * (M + 1))
                    for n in range(2):
                        cols = slice(n * N, (n + 1) * N)
                        link(nc.vector.scalar_tensor_tensor(work[:, b, cols], work[:, b, cols], rstd[:, 2, b:b + 1],
                                                            g_ple[:, cols], ALU.mult, ALU.mult))
                        nc.vector.tensor_tensor(resid[:, b, cols], resid[:, b, cols], work[:, b, cols], ALU.add)\
                            .then_inc(x2_done, 1)

        @block.tensor
        def _(pe):
            def wait_bank(L, chunk, n, b):
                prev = L - 1
                if chunk == "PLE":
                    if L > 0:
                        pe.wait_ge(wg_sig, prev * 4 + (1 if n == 0 else 3) + b)
                elif chunk == "IDX":
                    pe.wait_ge(ple_out, L * 4 + 2 + b + 1)
                elif chunk == "QB":
                    pe.wait_ge(ple_out, L * 4 + b + 1)
                elif chunk == "KB":
                    pe.wait_ge(idx_out, L * 2 + b + 1)
                elif chunk == "VB":
                    pe.wait_ge(z_out, L * 8 + b + 1)
                elif chunk == "QA":
                    pe.wait_ge(z_out, L * 8 + 2 + b + 1)
                elif chunk == "KA":
                    pe.wait_ge(v_out, L * 4 + b + 1)
                elif chunk == "VA":
                    pe.wait_ge(z_out, L * 8 + 4 + b + 1)
                elif chunk == "GA":
                    pe.wait_ge(z_out, L * 8 + 6 + b + 1)
                elif chunk == "GB":
                    pe.wait_ge(v_out, L * 4 + 2 + b + 1)
                elif chunk == "WO":
                    pe.wait_ge(glu_done, L * 4 + 2 * b + n + 1)
                else:
                    pe.wait_ge(wo_scaled, L * 4 + 2 * b + n + 1)

            def wait_tr(L, s):
                i = tr_index(L, s)
                if i > 1:
                    pe.wait_ge(tr_out, i - 1)

            pe.wait_ge(const_done, 2)
            for pos, (L, s) in enumerate(STEPS):
                kind = s[0]
                if kind == "mm":
                    u, b = s[1:]
                    g = L * U + u
                    chunk, n, k0, nk, cols = UNITS[u]
                    ps = proj[bank_of(chunk, n, b)][:, 0:cols]
                    if k0 == 0:
                        wait_bank(L, chunk, n, b)
                    pe.wait_ge(lo_done, g + 1)
                    if chunk == "PLE":
                        pe.wait_ge(p_lo_done, L + 1)
                        src_hi, src_lo = p_hi, p_lo
                    else:
                        src = "y" if chunk == "WO" else "x" if chunk == "WG" else "h"
                        pe.wait_ge(at_lo, L * 12 + t8_index(src, b, k0 // 4) + 1)
                        src_hi, src_lo = act_hi, act_lo
                    for k in range(nk):
                        hi = w_hi[:, g % SLOTS, k * cols:(k + 1) * cols]
                        lo = w_lo[:, g % SLOTS, k * cols:(k + 1) * cols]
                        last_k = u == LAST_OF[chunk, n] and k == nk - 1
                        nc.tensor.matmul(ps, src_hi[:, b, k0 + k, :], hi, start=(k0 + k == 0), stop=False)
                        nc.tensor.matmul(ps, src_hi[:, b, k0 + k, :], lo, start=False, stop=False)
                        last = nc.tensor.matmul(ps, src_lo[:, b, k0 + k, :], hi, start=False, stop=last_k)
                    if b == 1:
                        last.then_inc(unit_used, 1)
                    elif last_k:
                        last.then_inc(b0_done, 1)
                elif kind == "pT":
                    m = s[1]
                    pe.wait_ge(p_in[m], 16)
                    if m > 0:
                        pe.wait_ge(pv_out, m * 4)
                    for b in range(NB):
                        for k in range(D_PLE // P):
                            j = b * 2 + k
                            last = nc.tensor.transpose(pv[:, j * P:(j + 1) * P], p_raw[:, b, k * P:(k + 1) * P],
                                                       ident[:, :])
                    last.then_inc(ptr_done, 1)
                elif kind == "t8":
                    src, b, half = s[1:]
                    i = t8_index(src, b, half)
                    if src == "h":
                        pe.wait_ge(h_done, L * 2 + b + 1)
                    elif src == "y":
                        pe.wait_ge(y_done, L * 4 + 2 + b + 1)
                    else:
                        pe.wait_ge(x1_done, L * 2 + b + 1)
                    if i in (4, 5):
                        pe.wait_ge(exp_done, L * 12 + 7 + i)
                    elif L * 12 + i >= 2:
                        pe.wait_ge(at_lo, L * 12 + i - 1)
                    for j in range(4):
                        k = 4 * half + j
                        if src == "h":
                            tile = work[:, b, k * P:(k + 1) * P]
                        elif src == "y":
                            tile = y_mix[1 - half][b][:, j, :]
                        else:
                            tile = resid[:, b, k * P:(k + 1) * P]
                        last = nc.tensor.transpose(sc[half][:, j * P:(j + 1) * P], tile, ident[:, :])
                    last.then_inc(t8_done, 1)
                elif kind == "TI":
                    b = s[1]
                    wait_tr(L, s)
                    pe.wait_ge(rope_idx, L * 2 + b + 1)
                    for j in range(3):
                        last = nc.tensor.transpose(tr[:, j * P:(j + 1) * P], z_idx[:, b, j * P:(j + 1) * P],
                                                   ident[:, :])
                    last.then_inc(tr_done, 1)
                elif kind == "T":
                    chunk, b = s[1:]
                    wait_tr(L, s)
                    pe.wait_ge(rope_z, L * 8 + Z_ORDER.index(chunk) * 2 + b + 1)
                    z = z_view(chunk, b)
                    for j in range(4):
                        last = nc.tensor.transpose(tr[:, j * P:(j + 1) * P], z[:, j * P:(j + 1) * P], ident[:, :])
                    last.then_inc(tr_done, 1)
                elif kind == "D":
                    i = s[1]
                    b, odd = divmod(i, 2)
                    keys = (b + 1) * P
                    pe.wait_ge(tr_out, tr_index(L, ("TI", b)))
                    if i < 2:
                        pe.wait_ge(at_lo, L * 12 + 3 + i)
                    else:
                        pe.wait_ge(relu_done, L * 4 + i - 1)
                    rows = slice(odd * HEAD, (odd + 1) * HEAD)
                    for j in range(2):
                        last = nc.tensor.matmul(sc[i % 2][:, j * keys:(j + 1) * keys],
                                                idxT[rows, j, b * P:(b + 1) * P], idxT[rows, 2, 0:keys],
                                                start=True, stop=True)
                    last.then_inc(dots_done, 1)
                elif kind == "S":
                    i = s[1]
                    g, b, maps, keys = s_task(i)
                    pe.wait_ge(tr_out, tr_index(L, ("T", "KB" if g == 0 else "KA", b)))
                    if i < 2:
                        pe.wait_ge(relu_done, L * 4 + 3 + i)
                    else:
                        pe.wait_ge(exp_done, L * 12 + i - 1)
                    if g == 1:
                        pe.wait_ge(mask_done, L * 2 + b + 1)
                        mask, first = sel_mask[b], 0
                    else:
                        mask, first = causal, keys - CHUNK
                    for j, m in enumerate(maps):
                        rows = slice((m % 2) * HEAD, (m % 2 + 1) * HEAD)
                        ps = sc[i % 2][:, j * keys:(j + 1) * keys]
                        nc.tensor.matmul(ps, qT[g][rows, m // 2, b * P:(b + 1) * P], kT[rows, m // 2, 0:keys],
                                         start=True, stop=False)
                        last = nc.tensor.matmul(ps[:, first:keys], ident16[:, :], mask[:, 0:keys - first],
                                                start=False, stop=True)
                    last.then_inc(s_done, 1)
                elif kind == "PT":
                    n = s[1]
                    g, b, tiles = pt_task(n)
                    wait_tr(L, s)
                    if g == 0:
                        pe.wait_ge(mix_done, L * 3 + n + 1)
                    else:
                        pe.wait_ge(exp_done, L * 12 + tiles[0][2] + 1)
                    for j, (h, kt, si, col) in enumerate(tiles):
                        last = nc.tensor.transpose(tr[:, j * P:(j + 1) * P], probs[:, si % 4, col:col + P],
                                                   ident[:, :])
                    last.then_inc(tr_done, 1)
                elif kind == "PV":
                    n = s[1]
                    g, b, tiles = pt_task(n)
                    width = P if g == 0 else HEAD
                    pe.wait_ge(tr_out, tr_index(L, ("PT", n)))
                    pe.wait_ge(v_out, L * 4 + 2 * g + b + 1)
                    if n == 0:
                        pe.wait_ge(p_lo_done, L + 1)
                    for gi, (_, _, members) in enumerate(PV_GROUP):
                        if gi and n == members[0]:
                            pe.wait_ge(pv_out, L * 4 + gi)
                    for j, (h, kt, si, col) in enumerate(tiles):
                        last = nc.tensor.matmul(pv[:, h * width:(h + 1) * width], pT[:, n % 3, j, :],
                                                v_all[:, kt, g, h * width:(h + 1) * width], start=(kt == 0),
                                                stop=(kt == b))
                    last.then_inc(pv_done, 1)


_INS = ["x", "p", "pre_norm_g", "w_in", "w_out", "post_norm_g", "lambda_q1", "lambda_k1", "lambda_q2", "lambda_k2",
        "subln_g", "w_ple_gate", "w_ple_proj", "ple_norm_g"]


def kernel(**inputs):
    import numpy as _np
    import concourse.bacc as _bacc
    from concourse import mybir as _mybir
    from concourse.bass_utils import run_bass_kernel_spmd as _run

    nc = _bacc.Bacc("TRN2", target_bir_lowering=False, num_devices=1)
    arrays, args = {}, []
    for name in _INS:
        a = _np.ascontiguousarray(inputs[name])
        arrays[f"in_{name}_dram"] = a
        args.append(nc.dram_tensor(f"in_{name}_dram", a.shape, _mybir.dt.from_np(a.dtype), kind="ExternalInput").ap())
    f32 = _np.float32
    inv = f32(500000.0) ** (-_np.arange(0, ROT, 2, dtype=f32) / f32(ROT))
    angle = _np.arange(SEQ, dtype=f32)[:, None] * inv[None, :]
    table = _np.concatenate([_np.cos(angle), _np.cos(angle), -_np.sin(angle), _np.sin(angle)], axis=1).astype(f32)
    arrays["rope_dram"] = table
    args.append(nc.dram_tensor("rope_dram", table.shape, _mybir.dt.float32, kind="ExternalInput").ap())
    args.append(nc.dram_tensor("out_0_dram", (1, SEQ, D_MODEL), _mybir.dt.float32, kind="ExternalOutput").ap())
    build(nc, *args)
    r = _run(nc, [arrays], core_ids=[0])
    return r.results[0]["out_0_dram"]
```

```python
import math
from contextlib import ExitStack

import concourse.bass as bass
from concourse import mybir

DEPTH, SEQ, D_MODEL, D_PLE = 2, 256, 1024, 256
P = 128
NB = SEQ // P
KT = D_MODEL // P
HEAD = 64
CHUNK = 64
TOPK = min(256, SEQ // 4)
D_HALF = D_MODEL // 2
A_HEADS, B_HEADS, IDX_HEADS = 8, 4, 4
ROT = HEAD // 4
EPS = 1e-6
NEG = -1e30
INADMISSIBLE = -1e38
TAKEN = -3e38
IDX_W = IDX_HEADS * HEAD + HEAD + IDX_HEADS
N = 512

_sizes = [D_HALF, D_HALF, D_HALF, IDX_HEADS * HEAD, HEAD, IDX_HEADS, D_HALF, D_HALF, D_HALF, D_HALF, D_HALF]
_off = [sum(_sizes[:i]) for i in range(len(_sizes))]
COL = dict(QA=_off[0], KA=_off[1], VA=_off[2], IDX=_off[3], GA=_off[6], QB=_off[7], KB=_off[8], VB=_off[9],
           GB=_off[10])

KU = 2
IN_CHUNKS = ["IDX", "QB", "KB", "VB", "QA", "KA", "VA", "GA", "GB"]
UNITS = [("PLE", n, 0, KU, N) for n in range(2)]
for _c in IN_CHUNKS:
    UNITS += [(_c, 0, k, KU, IDX_W if _c == "IDX" else N) for k in range(0, KT, KU)]
for _c in ("WO", "WG"):
    UNITS += [(_c, n, k, KU, N) for n in range(2) for k in range(0, KT, KU)]
U = len(UNITS)
FIRST = {}
for _i, _u in enumerate(UNITS):
    FIRST.setdefault(_u[0], _i)
LAST_OF = {(_u[0], _u[1]): _i for _i, _u in enumerate(UNITS)}
UQ = KT // KU
B0_ORDER = [("PLE", 0), ("PLE", 1)] + [(c, 0) for c in IN_CHUNKS] + [("WO", 0), ("WO", 1), ("WG", 0), ("WG", 1)]
RAW_SLOTS, SLOTS = 5, 10
START = [1, 2, 5, 8, 11, 11, 16, 17, 18, 19]
HOLD = 2
LEAD, PACE = 8, 1.75
WARM = 4, 8
UE = KU * N


def layer_steps(L):
    out = []

    def mms(chunk, order, side):
        for i, (u, b) in enumerate(order):
            out.append(("mm", FIRST[chunk] + u, b))
            out.extend(side.get(i, ()))

    both = [(u, b) for u in range(UQ) for b in range(NB)]
    one = lambda b, n=UQ: [(u, b) for u in range(n)]
    ple = [(n, b) for n in range(2) for b in range(NB)]
    t8 = lambda src, b: [("t8", src, b, 0), ("t8", src, b, 1)]
    if L == 0:
        out += [("pT", 0), ("pre", 0, 0)]
        mms("PLE", ple, {0: [("pre", 1, 0)], 2: t8("h", 0), 3: t8("h", 1)})
        mms("IDX", both, {})
        mms("QB", both, {3: [("TI", 0)], 5: [("D", 0)], 6: [("D", 1)]})
    else:
        out += [("ple0", 1, 1, L - 1)]
        mms("PLE", ple, {0: t8("h", 0) + [("psq", 1, 1, L - 1), ("ple1", 1, L - 1)], 2: [("pre", 1, L)]})
        mms("IDX", one(0), {})
        mms("QB", one(0), {1: t8("h", 1)})
        mms("IDX", one(1), {})
        mms("QB", one(1), {1: [("TI", 0)], 2: [("D", 0)], 3: [("D", 1)]})
    mid = [[] for _ in range(6 * len(both))]
    placed = [(0, ("TI", 1)), (2, ("D", 2)), (3, ("T", "QB", 0)), (4, ("D", 3)), (5, ("T", "QB", 1)), (5, ("lam",)),
              (11, ("T", "KB", 0)), (13, ("T", "KB", 1)), (25, ("T", "QA", 0)), (28, ("T", "QA", 1)),
              (33, ("T", "KA", 0)), (36, ("T", "KA", 1))]
    for n, i in enumerate([12, 14, 16, 18, 20, 22, 35, 36, 38, 39, 41, 43]):
        placed += [(i, ("S", n)), (i, ("E", n))]
    placed += [(i, ("R", n)) for n, i in enumerate([13, 15, 17, 19, 21, 23, 37, 38, 39, 40, 42, 44])]
    placed += [(i, ("PT", n)) for n, i in enumerate([18, 22, 26, 38, 40, 42, 43, 44, 45])]
    placed += [(i, ("PV", n)) for n, i in enumerate([19, 24, 28, 41, 42, 43, 44, 45, 46])]
    placed += [(20, ("hv", 0)), (22, ("hn", 0)), (29, ("hv", 1)), (31, ("hn", 1))]
    placed += [(i, ("topk", 0, r)) for r, i in enumerate([1, 2, 3, 4, 5, 6, 7, 8])]
    placed += [(i, ("topk", 1, r)) for r, i in enumerate([9, 24, 25, 26, 27, 29, 31, 32])]
    rank = {"PV": 1, "PT": 2, "T": 3, "TI": 3, "D": 3, "S": 4, "E": 5, "hv": 6, "hn": 7, "R": 8, "topk": 9,
            "lam": 10}
    for i, step in sorted(placed, key=lambda q: (q[0], rank[q[1][0]], q[1][1:])):
        mid[i].append(step)
    for c, chunk in enumerate(["KB", "VB", "QA", "KA", "VA", "GA"]):
        mms(chunk, both, dict(enumerate(mid[c * len(both):(c + 1) * len(both)])))
    mms("GB", one(0), {})
    mms("GB", one(1), {2: t8("y", 0)})
    mixed = [(u, 0) for u in (0, 1, 2, 3, 4)] + [(u, 1) for u in (0, 1)] + [(u, 0) for u in (5, 6, 7)] \
        + [(u, 1) for u in (2, 3, 4, 5, 6, 7)]
    mms("WO", mixed, {3: t8("y", 1), 4: [("post0", 0, 0)], 10: [("post0", 0, 1)], 11: [("post1", 0), ("post0", 1, 0)],
                      14: t8("x", 0) + ([("pT", L + 1)] if L + 1 < DEPTH else [])})
    mms("WG", mixed, {0: [("post0", 1, 1)], 1: [("post1", 1)], 3: t8("x", 1), 4: [("ple0", 0, 0, L), ("psq", 0, 0, L)],
                      10: [("ple0", 0, 1, L), ("psq", 0, 1, L)], 11: [("ple1", 0, L), ("ple0", 1, 0, L)],
                      12: ([("pre", 0, L + 1)] if L + 1 < DEPTH else []) + [("psq", 1, 0, L)]})
    if L + 1 == DEPTH:
        out += [("ple0", 1, 1, L), ("psq", 1, 1, L), ("ple1", 1, L)]
    return out


def all_steps():
    steps = [(L, s) for L in range(DEPTH) for s in layer_steps(L)]
    pieces = [pos for pos, (L, s) in enumerate(steps) if s[0] == "mm"]
    first_use, last_use = {}, {}
    held = set()
    for i, pos in enumerate(pieces):
        L, (_, u, b) = steps[pos]
        first_use.setdefault(L * U + u, i)
        last_use[L * U + u] = i
        if L and u < 2 and i - first_use[L * U] < HOLD:
            held.add(i)
    latest = {}
    for g in reversed(range(DEPTH * U)):
        latest[g] = min(first_use[g] - LEAD, latest.get(g + 1, 10 ** 6) - PACE)
    high, low = [[] for _ in steps], [[] for _ in steps]
    at = 0
    for g in range(DEPTH * U):
        if g < len(START):
            pos = START[g]
        else:
            at = max(at + 1, int(latest[g]), last_use[g - SLOTS] + 1)
            while at in held:
                at += 1
            pos = pieces[at]
        high[pos].append(g)
        low[pos if g < SLOTS else pieces[at + 1]].append(g)
        if g < len(START):
            at = max(i for i, q in enumerate(pieces) if q <= max(pos, pieces[0]))
    return steps, high, low


def build(nc, x, p, pre_norm_g, w_in, w_out, post_norm_g, lambda_q1, lambda_k1, lambda_q2, lambda_k2, subln_g,
          w_ple_gate, w_ple_proj, ple_norm_g, rope, out):
    fp32, f32r, bf16 = mybir.dt.float32, mybir.dt.float32r, mybir.dt.bfloat16
    ALU, ACT, AX = mybir.AluOpType, mybir.ActivationFunctionType, mybir.AxisListType
    STEPS, HIGH, LOW = all_steps()

    ctx = ExitStack()
    with ctx:
        def sb(name, shape, dt=fp32):
            return ctx.enter_context(nc.sbuf_tensor(name, shape, dt))

        def sem(name):
            return ctx.enter_context(nc.semaphore(name))

        raw = sb("raw", [P, RAW_SLOTS, UE])
        w_hi = sb("w_hi", [P, SLOTS, UE], f32r)
        w_lo = sb("w_lo", [P, SLOTS, UE], f32r)
        resid = sb("resid", [P, NB, D_MODEL])
        work = sb("work", [P, NB, D_MODEL])
        act_hi = sb("act_hi", [P, NB, KT, P], f32r)
        act_lo = sb("act_lo", [P, NB, KT, P], f32r)
        p_raw = sb("p_raw", [P, NB, D_PLE])
        p_hi = sb("p_hi", [P, NB, D_PLE // P, P], f32r)
        p_lo = sb("p_lo", [P, NB, D_PLE // P, P], f32r)
        emb = sb("emb", [P, NB, D_MODEL])
        v_all = sb("v_all", [P, NB, 2, D_HALF])
        z_idx = v_all[:, :, 0, 0:6 * HEAD]
        gate = sb("gate", [P, NB, D_HALF])
        qT = [sb("qT_b", [P, 4, SEQ]), sb("qT_a", [P, 4, SEQ])]
        kT = sb("kT", [P, 4, P])
        k_hi = sb("k_hi", [P, 4, SEQ], f32r)
        k_lo = sb("k_lo", [P, 4, SEQ], f32r)
        q_hi = sb("q_hi", [P, 4, P], f32r)
        q_lo = sb("q_lo", [P, 4, P], f32r)
        y_mix = [[qT[g][:, :, b * P:(b + 1) * P] for b in range(NB)] for g in range(2)]
        e_g = [qT[b][:, :, :].rearrange("p j t -> p (j t)") for b in range(NB)]
        probs = sb("probs", [P, 4, N])
        pT = sb("pT", [P, 3, 4, P])
        idxT = pT[:, 0:2, :, :].rearrange("p a t q -> p (a t q)")[:, 0:3 * SEQ].rearrange("p (j t) -> p j t", j=3)
        score = [sb("score0", [P, P]), sb("score1", [P, SEQ])]
        sel_mask = [sb("sel_mask0", [P, P], bf16), sb("sel_mask1", [P, SEQ], bf16)]
        causal = sb("causal", [P, CHUNK], bf16)
        ident = sb("ident", [P, P])
        ident16 = sb("ident16", [P, P], bf16)
        g_norm = sb("g_norm", [P, D_MODEL])
        g_ple = sb("g_ple", [P, D_MODEL])
        g_sub = sb("g_sub", [P, P])
        lam_in = sb("lam_in", [P, 4, HEAD])
        lam_s = sb("lam_s", [P, 2])
        lam_e = sb("lam_e", [P, 2])
        neg_lam = sb("neg_lam", [P, 1])
        rot_tab = sb("rot_tab", [P, NB, 2 * ROT])
        cos2, sin2 = rot_tab[:, :, 0:ROT], rot_tab[:, :, ROT:2 * ROT]
        rot_a, rot_b = (v_all[:, 0, 1, i * 8 * ROT:(i + 1) * 8 * ROT].rearrange("p (h r) -> p h r", r=ROT)
                        for i in range(2))
        w_idx = sb("w_idx", [P, NB, IDX_HEADS])
        top8 = sb("top8", [P, 8])
        neg_max = sb("neg_max", [P, 2, 4])
        row_sum = sb("row_sum", [P, 2, NB, 8])
        row_rec = sb("row_rec", [P, 2, NB, 8])
        mix_c = sb("mix_c", [P, 4])
        ssq = sb("ssq", [P, 3, NB, 2])
        var = sb("var", [P, 3, NB])
        rstd = sb("rstd", [P, 3, NB])
        ssq_h = sb("ssq_h", [P, NB, B_HEADS])
        var_h = sb("var_h", [P, NB, B_HEADS])
        rstd_h = sb("rstd_h", [P, NB, B_HEADS])
        scale_h = sb("scale_h", [P, NB, B_HEADS])
        minus_half = sb("minus_half", [P, B_HEADS])

        proj = [ctx.enter_context(nc.psum_tensor(f"proj{i}", [P, N], fp32)) for i in range(4)]
        sc = [ctx.enter_context(nc.psum_tensor(f"sc{i}", [P, N], fp32)) for i in range(2)]
        tr = ctx.enter_context(nc.psum_tensor("tr", [P, N], fp32))
        pv = ctx.enter_context(nc.psum_tensor("pv", [P, N], fp32))

        raw_in = [sem(f"raw_in{i}") for i in range(RAW_SLOTS)]
        hi_done, lo_done = sem("hi_done"), sem("lo_done")
        unit_used = sem("unit_used")
        b0_done = sem("b0_done")
        x_in = [sem(f"x_in{b}") for b in range(NB)]
        p_in = [sem(f"p_in{L}") for L in range(DEPTH)]
        gpre_in = [sem(f"gpre_in{L}") for L in range(DEPTH)]
        rope_in, gpost_in, gple_in, small_in = (sem(n) for n in ("rope_in", "gpost_in", "gple_in", "small_in"))
        const_done = sem("const_done")
        sq_done = [sem(f"sq_done{i}") for i in range(3)]
        var_done = [sem(f"var_done{i}") for i in range(3)]
        rstd_done = [sem(f"rstd_done{i}") for i in range(3)]
        h_done, x1_done, x2_done = sem("h_done"), sem("x1_done"), sem("x2_done")
        t8_done, at_hi, at_lo = sem("t8_done"), sem("at_hi"), sem("at_lo")
        ptr_done, p_hi_done, p_lo_done = sem("ptr_done"), sem("p_hi_done"), sem("p_lo_done")
        ple_out = sem("ple_out")
        idx_out, z_out, v_out = sem("idx_out"), sem("z_out"), sem("v_out")
        rope_idx, rope_z = sem("rope_idx"), sem("rope_z")
        tr_done, tr_out = sem("tr_done"), sem("tr_out")
        qk_hi_done = sem("qk_hi_done")
        dots_done, relu_done, score_done = sem("dots_done"), sem("relu_done"), sem("score_done")
        mask_done = sem("mask_done")
        s_done, max_done, exp_done, mix_done = (sem(n) for n in ("s_done", "max_done", "exp_done", "mix_done"))
        rec_done = sem("rec_done")
        pv_done, pv_out = sem("pv_done"), sem("pv_out")
        sqh_done, varh_done, rstdh_done = sem("sqh_done"), sem("varh_done"), sem("rstdh_done")
        sig_done, glu_done, y_done = sem("sig_done"), sem("glu_done"), sem("y_done")
        wo_scaled, wg_sig, e_done = sem("wo_scaled"), sem("wg_sig"), sem("e_done")
        lam_sum, lam_exp, lam_done = sem("lam_sum"), sem("lam_exp"), sem("lam_done")
        dve_chain, pool_chain = sem("dve_chain"), sem("pool_chain")
        stored = sem("stored")

        def bank_of(chunk, n, b):
            if chunk == "PLE":
                return 2 * (1 - n) + b
            if chunk in ("WO", "WG"):
                return (2 if b == 0 else 0) + n
            return 2 * (IN_CHUNKS.index(chunk) % 2) + b

        def wait_sum(eng, L, chunk, n, b):
            if b == 0:
                eng.wait_ge(b0_done, L * len(B0_ORDER) + B0_ORDER.index((chunk, n)) + 1)
            else:
                eng.wait_ge(unit_used, L * U + LAST_OF[chunk, n] + 1)

        Z_ORDER = ["QB", "KB", "QA", "KA"]

        def z_view(chunk, b):
            half = Z_ORDER.index(chunk) % 2
            return work[:, b, half * N:(half + 1) * N]

        tr_steps = [s for s in layer_steps(0) if s[0] in ("TI", "T", "PT")]
        TRN = len(tr_steps)

        QK_WHOLE = [("QB", 0), ("QA", 0)]
        QK_SPLIT = [s[1:] for s in tr_steps if s[0] == "T" and s[1:] not in QK_WHOLE]

        def tr_index(L, s):
            return L * TRN + tr_steps.index(s) + 1

        def s_task(i):
            g, r = divmod(i, 6)
            if r < 2:
                return g, 0, list(range(r, 8, 2)), P
            q, odd = divmod(r - 2, 2)
            return g, 1, [4 * q + odd, 4 * q + odd + 2], SEQ

        def pt_task(n):
            si = [0, 2, 4, 6, 7, 8, 9, 10, 11][n]
            g, b, maps, keys = s_task(si)
            return g, b, [(m // 2 if g == 0 else m, kt, si, j * keys + kt * P)
                          for j, m in enumerate(maps) for kt in range(b + 1)]

        PT_OF_S = {}
        for n_ in range(9):
            for _, _, s_, _ in pt_task(n_)[2]:
                PT_OF_S[s_] = n_
        PV_GROUP = [(0, 0, [0]), (0, 1, [1, 2]), (1, 0, [3, 4]), (1, 1, [5, 6, 7, 8])]

        T8_BASE = dict(h=0, y=4, x=8)

        def t8_index(kind, b, half):
            return T8_BASE[kind] + 2 * b + half

        block = ctx.enter_context(nc.Block())

        @block.sync
        def _(sp):
            def load_x(b):
                sp.dma_start(resid[:, b, :], x[0, b * P:(b + 1) * P, :]).then_inc(x_in[b], 16)

            sp.dma_start(p_raw[:, :, :], p[0, 0].rearrange("(b p) d -> p b d", p=P)).then_inc(p_in[0], 16)
            for g in range(DEPTH * U):
                L, u = divmod(g, U)
                chunk, n, k0, nk, cols = UNITS[u]
                if chunk == "PLE":
                    src = w_ple_proj[L, :, n * N:(n + 1) * N]
                elif chunk == "WO":
                    src = w_out[L, k0 * P:(k0 + nk) * P, n * N:(n + 1) * N]
                elif chunk == "WG":
                    src = w_ple_gate[L, k0 * P:(k0 + nk) * P, n * N:(n + 1) * N]
                else:
                    src = w_in[L, k0 * P:(k0 + nk) * P, COL[chunk]:COL[chunk] + cols]
                if g >= RAW_SLOTS:
                    sp.wait_ge(lo_done, g - RAW_SLOTS + 1)
                sp.dma_start(raw[:, g % RAW_SLOTS, 0:nk * cols].rearrange("p (k n) -> p k n", k=nk),
                             src.rearrange("(k p) n -> p k n", p=P)).then_inc(raw_in[g % RAW_SLOTS], 16)
                if g == 0:
                    load_x(0)
                elif g == 1:
                    sp.dma_start(g_norm[:, :], pre_norm_g[0, :].partition_broadcast(P)).then_inc(gpre_in[0], 16)
                    load_x(1)
                elif g == 2:
                    sp.dma_start(rot_tab[:, :, :], rope.rearrange("(b p) r -> p b r", p=P)).then_inc(rope_in, 16)
            for i in range(2 * NB):
                b, n = divmod(i, 2)
                sp.wait_ge(x2_done, (DEPTH - 1) * 4 + i + 1)
                sp.dma_start(out[0, b * P:(b + 1) * P, n * N:(n + 1) * N], resid[:, b, n * N:(n + 1) * N])\
                    .then_inc(stored, 16)
            sp.wait_ge(stored, 16 * 2 * NB)

        @block.gpsimd
        def _(pool):
            chain = [0]

            def link(ins):
                chain[0] += 1
                ins.then_inc(pool_chain, 1)
                pool.wait_ge(pool_chain, chain[0])

            def bcast(vec):
                return vec.partition_broadcast(P)

            def load_p(L):
                pool.dma_start(p_raw[:, :, :], p[L, 0].rearrange("(b p) d -> p b d", p=P)).then_inc(p_in[L], 16)

            def load_small(L):
                for i, v in enumerate((lambda_q1, lambda_q2, lambda_k1, lambda_k2)):
                    pool.dma_start(lam_in[:, i, :], bcast(v[L, :])).then_inc(small_in, 16)
                pool.dma_start(g_sub[:, :], bcast(subln_g[L, :])).then_inc(small_in, 16)

            nc.gpsimd.memset(minus_half[:, :], -0.5)
            link(nc.gpsimd.memset(ident[:, :], 0.0))
            link(nc.gpsimd.affine_select(out=ident[:, :], in_=ident[:, :], compare_op=ALU.not_equal, fill=1.0, base=0,
                                         pattern=[[-1, P]], channel_multiplier=1))
            nc.gpsimd.tensor_copy(ident16[:, :], ident[:, :]).then_inc(const_done, 1)
            link(nc.gpsimd.memset(causal[:, :], 0.0))
            nc.gpsimd.memset(causal[0:CHUNK, :], NEG).then_inc(const_done, 1)

            rot_user = [None]

            def rope_rows(view, heads, b, done, value):
                if rot_user[0]:
                    pool.wait_ge(*rot_user[0])
                rot_user[0] = (done, value)
                lo_half, hi_half = view[:, :, 0:ROT // 2], view[:, :, ROT // 2:ROT]

                def table(t, cols):
                    return t[:, b:b + 1, cols].to_broadcast([P, heads, cols.stop - cols.start])

                nc.gpsimd.tensor_tensor(rot_a[:, 0:heads, :], view[:, :, 0:ROT], table(cos2, slice(0, ROT)), ALU.mult)
                nc.gpsimd.tensor_tensor(rot_b[:, 0:heads, 0:ROT // 2], hi_half, table(sin2, slice(0, ROT // 2)),
                                        ALU.mult)
                link(nc.gpsimd.tensor_tensor(rot_b[:, 0:heads, ROT // 2:ROT], lo_half,
                                             table(sin2, slice(ROT // 2, ROT)), ALU.mult))
                nc.gpsimd.tensor_tensor(view[:, :, 0:ROT], rot_a[:, 0:heads, :], rot_b[:, 0:heads, :],
                                        ALU.add).then_inc(done, 1)

            def inv_sqrt(i, L, b):
                pool.wait_ge(var_done[i], L * 2 + b + 1)
                nc.gpsimd.tensor_tensor(rstd[:, i, b:b + 1], var[:, i, b:b + 1], minus_half[:, 0:1],
                                        ALU.pow).then_inc(rstd_done[i], 1)

            for pos, (L, s) in enumerate(STEPS):
                kind = s[0]
                if kind == "mm":
                    chunk, n, k0, nk, cols = UNITS[s[1]]
                    b = s[2]
                    if s[1] != LAST_OF[chunk, n]:
                        continue
                    if chunk == "IDX":
                        pool.wait_ge(rope_in, 16)
                        pool.wait_ge(idx_out, L * 2 + b + 1)
                        rope_rows(z_idx[:, b, :].rearrange("p (h d) -> p h d", d=HEAD), 6, b, rope_idx,
                                  L * 2 + b + 1)
                    elif chunk in Z_ORDER:
                        pool.wait_ge(z_out, L * 8 + Z_ORDER.index(chunk) * 2 + b + 1)
                        rope_rows(z_view(chunk, b).rearrange("p (h d) -> p h d", d=HEAD), 8, b, rope_z,
                                  L * 8 + Z_ORDER.index(chunk) * 2 + b + 1)
                elif kind == "hv":
                    b = s[1]
                    pool.wait_ge(varh_done, L * 2 + b + 1)
                    nc.gpsimd.tensor_tensor(rstd_h[:, b, :], var_h[:, b, :], minus_half[:, :], ALU.pow)\
                        .then_inc(rstdh_done, 1)
                elif kind == "pre":
                    inv_sqrt(0, s[2], s[1])
                elif kind == "post1":
                    inv_sqrt(1, L, s[1])
                elif kind == "ple1":
                    inv_sqrt(2, s[2], s[1])
                if kind == "t8" and s[1:] == ("h", 1, 1) and L + 1 < DEPTH or kind == "pT" and 0 < s[1] < DEPTH - 1:
                    m = L if kind == "t8" else s[1]
                    pool.wait_ge(ptr_done, m + 1)
                    load_p(m + 1)
                if kind == "t8" and s[1:] == ("h", 1, 1):
                    pool.wait_ge(h_done, L * 2 + 2)
                    pool.dma_start(g_norm[:, :], bcast(post_norm_g[L, :])).then_inc(gpost_in, 16)
                    if L == 0:
                        load_small(0)
                        pool.dma_start(g_ple[:, :], bcast(ple_norm_g[0, :])).then_inc(gple_in, 16)
                if kind == "post1" and s[1] == 1 and L + 1 < DEPTH:
                    pool.wait_ge(x1_done, L * 2 + 2)
                    pool.dma_start(g_norm[:, :], bcast(pre_norm_g[L + 1, :])).then_inc(gpre_in[L + 1], 16)
                    load_small(L + 1)
                if kind == "ple1" and s[1] == 1 and s[2] + 1 < DEPTH:
                    pool.wait_ge(x2_done, s[2] * 4 + 4)
                    pool.dma_start(g_ple[:, :], bcast(ple_norm_g[s[2] + 1, :])).then_inc(gple_in, 16)

        @block.scalar
        def _(act):
            def copy(dst, src, scale=1.0):
                return nc.scalar.activation(dst, src, ACT.Copy, scale=scale)

            def square_resid(L, b):
                nc.scalar.activation(work[:, b, :], resid[:, b, :], ACT.Square, scale=D_MODEL ** -0.5,
                                     accum_out=ssq[:, 0, b, 0:1]).then_inc(sq_done[0], 1)

            act.wait_ge(const_done, 2)
            copy(lam_e[:, :], minus_half[:, 0:2])
            for pos, (L, s) in enumerate(STEPS):
                for g in HIGH[pos]:
                    nk, cols = UNITS[g % U][3:]
                    act.wait_ge(raw_in[g % RAW_SLOTS], 16 * (g // RAW_SLOTS + 1))
                    if g >= SLOTS:
                        act.wait_ge(unit_used, g - SLOTS + 1)
                    copy(w_hi[:, g % SLOTS, 0:nk * cols], raw[:, g % RAW_SLOTS, 0:nk * cols]).then_inc(hi_done, 1)
                kind = s[0]
                if kind == "mm":
                    chunk, n, k0, nk, cols = UNITS[s[1]]
                    b = s[2]
                    if s[1] != LAST_OF[chunk, n] or chunk in ("WO", "WG"):
                        continue
                    ps = proj[bank_of(chunk, n, b)]
                    wait_sum(act, L, chunk, n, b)
                    if chunk == "PLE":
                        if L > 0:
                            act.wait_ge(e_done, (L - 1) * 4 + 2 * b + n + 1)
                        copy(emb[:, b, n * N:(n + 1) * N], ps[:, :]).then_inc(ple_out, 1)
                    elif chunk == "IDX":
                        nqk = 5 * HEAD
                        copy(z_idx[:, b, 0:nqk], ps[:, 0:nqk])
                        copy(z_idx[:, b, nqk:nqk + HEAD], ps[:, 4 * HEAD:nqk])
                        copy(w_idx[:, b, :], ps[:, nqk:nqk + IDX_HEADS], IDX_HEADS ** -0.5).then_inc(idx_out, 1)
                    elif chunk in Z_ORDER:
                        copy(z_view(chunk, b), ps[:, :]).then_inc(z_out, 1)
                    elif chunk in ("VB", "VA"):
                        copy(v_all[:, b, int(chunk == "VA"), :], ps[:, :]).then_inc(v_out, 1)
                    else:
                        if chunk == "GB":
                            act.wait_ge(y_done, L * 4 + b + 1)
                        else:
                            if L > 0:
                                act.wait_ge(y_done, (L - 1) * 4 + 2 + b + 1)
                        nc.scalar.activation(gate[:, b, :], ps[:, :], ACT.Sigmoid).then_inc(sig_done, 1)
                elif kind == "pT":
                    m = s[1]
                    act.wait_ge(ptr_done, m + 1)
                    copy(p_hi[:, :, :, :].rearrange("p b k t -> p (b k t)"), pv[:, :]).then_inc(p_hi_done, 1)
                elif kind == "pre":
                    b, M = s[1:]
                    if M == 0:
                        act.wait_ge(x_in[b], 16)
                    else:
                        act.wait_ge(x2_done, (M - 1) * 4 + 2 * b + 2)
                    square_resid(M, b)
                elif kind == "t8":
                    i = t8_index(s[1], s[2], s[3])
                    act.wait_ge(t8_done, L * 12 + i + 1)
                    copy(act_hi[:, s[2], 4 * s[3]:4 * s[3] + 4, :].rearrange("p k t -> p (k t)"),
                         sc[s[3]][:, :]).then_inc(at_hi, 1)
                elif kind == "TI":
                    b = s[1]
                    act.wait_ge(tr_done, tr_index(L, s))
                    copy(idxT[:, :, b * P:(b + 1) * P], tr[:, 0:3 * P].rearrange("p (j t) -> p j t", j=3))\
                        .then_inc(tr_out, 1)
                elif kind == "T":
                    chunk, b = s[1:]
                    act.wait_ge(tr_done, tr_index(L, s))
                    g, src = int(chunk[1] == "A"), tr[:, :].rearrange("p (j t) -> p j t", j=4)
                    if chunk[0] == "Q" and b == 0:
                        copy(qT[g][:, :, 0:P], src, HEAD ** -0.5).then_inc(tr_out, 1)
                    elif chunk[0] == "Q":
                        copy(q_hi[:, :, :], src, HEAD ** -0.5).then_inc(qk_hi_done, 1)
                    else:
                        if b == 0:
                            copy(kT[:, :, :], src)
                        copy(k_hi[:, :, b * P:(b + 1) * P], src).then_inc(qk_hi_done, 1)
                elif kind == "D":
                    i = s[1]
                    act.wait_ge(dots_done, L * 4 + i + 1)
                    w = 2 * P * (i // 2 + 1)
                    nc.scalar.activation(probs[:, i, 0:w], sc[i % 2][:, 0:w], ACT.Relu, scale=HEAD ** -0.5)\
                        .then_inc(relu_done, 1)
                elif kind == "E":
                    i = s[1]
                    g, b, maps, keys = s_task(i)
                    act.wait_ge(max_done, L * 12 + i + 1)
                    if i < 4:
                        act.wait_ge(score_done, L * 2 + i // 2 + 1)
                    elif i - 4 in PT_OF_S:
                        act.wait_ge(tr_done, tr_index(L, ("PT", PT_OF_S[i - 4])))
                    else:
                        act.wait_ge(mix_done, L * 3 + (i - 4) // 2 + 1)
                    for j, m in enumerate(maps):
                        last = nc.scalar.activation(probs[:, i % 4, j * keys:(j + 1) * keys],
                                                    sc[i % 2][:, j * keys:(j + 1) * keys], ACT.Exp,
                                                    bias=neg_max[:, i % 2, j:j + 1],
                                                    accum_out=row_sum[:, g, b, m:m + 1])
                    last.then_inc(exp_done, 1)
                elif kind == "PT":
                    n = s[1]
                    act.wait_ge(tr_done, tr_index(L, s))
                    if n >= 3:
                        act.wait_ge(pv_done, L * 9 + n - 2)
                    copy(pT[:, n % 3, :, :].rearrange("p t q -> p (t q)"), tr[:, :]).then_inc(tr_out, 1)
                elif kind == "PV":
                    for g, b, members in PV_GROUP:
                        if g == 0 and s[1] == members[-1]:
                            act.wait_ge(pv_done, L * 9 + members[-1] + 1)
                            act.wait_ge(mix_done, L * 3 + (1 if b == 0 else 3))
                            for h in range(B_HEADS):
                                last = nc.scalar.activation(y_mix[0][b][:, h, :], pv[:, h * P:(h + 1) * P],
                                                            ACT.Square, scale=row_rec[:, 0, b, 2 * h:2 * h + 1],
                                                            accum_out=ssq_h[:, b, h:h + 1])
                            last.then_inc(sqh_done, 1)
                elif kind == "post0":
                    b, n = s[1:]
                    wait_sum(act, L, "WO", n, b)
                    if b == 1:
                        act.wait_ge(sq_done[1], L * 4 + n + 1)
                    nc.scalar.activation(gate[:, n, :], proj[bank_of("WO", n, b)][:, :], ACT.Square,
                                         scale=D_MODEL ** -0.5, accum_out=ssq[:, 1, b, n:n + 1]).then_inc(sq_done[1], 1)
                elif kind == "ple0":
                    b, n, M = s[1:]
                    wait_sum(act, M, "WG", n, b)
                    half = work[:, b, n * N:(n + 1) * N]
                    nc.scalar.activation(half, proj[bank_of("WG", n, b)][:, :], ACT.Sigmoid).then_inc(wg_sig, 1)
                elif kind == "psq":
                    b, n, M = s[1:]
                    half = work[:, b, n * N:(n + 1) * N]
                    act.wait_ge(e_done, M * 4 + 2 * b + n + 1)
                    if 2 * b + n:
                        act.wait_ge(sq_done[2], M * 4 + 2 * b + n)
                    nc.scalar.activation(gate[:, 1, :], half, ACT.Square, scale=D_MODEL ** -0.5,
                                         accum_out=ssq[:, 2, b, n:n + 1]).then_inc(sq_done[2], 1)
                elif kind == "lam":
                    act.wait_ge(lam_sum, L + 1)
                    nc.scalar.activation(lam_e[:, :], lam_s[:, :], ACT.Exp).then_inc(lam_exp, 1)

        @block.vector
        def _(dve):
            chain = [0]

            def link(ins):
                chain[0] += 1
                ins.then_inc(dve_chain, 1)
                dve.wait_ge(dve_chain, chain[0])

            def lambda_of(L):
                lam_init = 0.8 - 0.6 * math.exp(-0.3 * L)
                dve.wait_ge(small_in, 16 * 5 * (L + 1))
                link(nc.vector.tensor_tensor(lam_in[:, 0:2, :], lam_in[:, 0:2, :], lam_in[:, 2:4, :], ALU.mult))
                nc.vector.tensor_reduce(lam_s[:, :], lam_in[:, 0:2, :], AX.X, ALU.add).then_inc(lam_sum, 1)
                nc.vector.tensor_scalar(g_sub[:, :], g_sub[:, :], 1.0 - lam_init, None, ALU.mult)
                dve.wait_ge(lam_exp, L + 1)
                nc.vector.tensor_scalar(neg_lam[:, :], lam_e[:, 1:2], lam_e[:, 0:1], -lam_init, ALU.subtract, ALU.add)\
                    .then_inc(lam_done, 1)

            def add_eps(i, L, b, parts):
                dve.wait_ge(sq_done[i], parts * (L * 2 + b + 1))
                if parts == 2:
                    nc.vector.tensor_scalar(var[:, i, b:b + 1], ssq[:, i, b, 0:1], ssq[:, i, b, 1:2], EPS, ALU.add,
                                            ALU.add).then_inc(var_done[i], 1)
                else:
                    nc.vector.tensor_scalar(var[:, i, b:b + 1], ssq[:, i, b, 0:1], EPS, None, ALU.add)\
                        .then_inc(var_done[i], 1)

            for pos, (L, s) in enumerate(STEPS):
                for g in LOW[pos]:
                    nk, cols = UNITS[g % U][3:]
                    dve.wait_ge(hi_done, g + 1)
                    nc.vector.tensor_tensor(w_lo[:, g % SLOTS, 0:nk * cols], raw[:, g % RAW_SLOTS, 0:nk * cols],
                                            w_hi[:, g % SLOTS, 0:nk * cols].bitcast(fp32), ALU.subtract)\
                        .then_inc(lo_done, 1)
                kind = s[0]
                if kind == "mm":
                    chunk, n, k0, nk, cols = UNITS[s[1]]
                    b = s[2]
                    if s[1] != LAST_OF[chunk, n] or chunk not in ("GA", "GB"):
                        continue
                    g = int(chunk == "GA")
                    i = L * 4 + (0 if g else 2) + b + 1
                    dve.wait_ge(sig_done, i)
                    nc.vector.tensor_tensor(gate[:, b, :], proj[bank_of(chunk, n, b)][:, :], gate[:, b, :], ALU.mult)\
                        .then_inc(glu_done, 1)
                    dve.wait_ge(glu_done, i)
                    dve.wait_ge(pv_out, L * 4 + 2 * g + b + 1)
                    nc.vector.tensor_tensor(y_mix[g][b], y_mix[g][b],
                                            gate[:, b, :].rearrange("p (j t) -> p j t", j=4), ALU.mult)\
                        .then_inc(y_done, 1)
                elif kind == "pT":
                    m = s[1]
                    dve.wait_ge(p_hi_done, m + 1)
                    nc.vector.tensor_tensor(p_lo[:, :, :, :].rearrange("p b k t -> p (b k t)"), pv[:, :],
                                            p_hi[:, :, :, :].rearrange("p b k t -> p (b k t)").bitcast(fp32),
                                            ALU.subtract).then_inc(p_lo_done, 1)
                elif kind == "pre":
                    b, M = s[1:]
                    add_eps(0, M, b, 1)
                    dve.wait_ge(rstd_done[0], M * 2 + b + 1)
                    dve.wait_ge(gpre_in[M], 16)
                    nc.vector.scalar_tensor_tensor(work[:, b, :], resid[:, b, :], rstd[:, 0, b:b + 1], g_norm[:, :],
                                                   ALU.mult, ALU.mult).then_inc(h_done, 1)
                elif kind == "t8":
                    i = t8_index(s[1], s[2], s[3])
                    dve.wait_ge(at_hi, L * 12 + i + 1)
                    nc.vector.tensor_tensor(act_lo[:, s[2], 4 * s[3]:4 * s[3] + 4, :].rearrange("p k t -> p (k t)"),
                                            sc[s[3]][:, :],
                                            act_hi[:, s[2], 4 * s[3]:4 * s[3] + 4, :].rearrange("p k t -> p (k t)")
                                            .bitcast(fp32), ALU.subtract).then_inc(at_lo, 1)
                elif kind == "T" and s[1:] not in QK_WHOLE:
                    chunk, b = s[1:]
                    src = tr[:, :].rearrange("p (j t) -> p j t", j=4)
                    dve.wait_ge(qk_hi_done, L * 6 + QK_SPLIT.index(s[1:]) + 1)
                    if chunk[0] == "Q":
                        ins = nc.vector.scalar_tensor_tensor(q_lo[:, :, :], src, HEAD ** -0.5,
                                                             q_hi[:, :, :].bitcast(fp32), ALU.mult,
                                                             ALU.subtract)
                    else:
                        ins = nc.vector.tensor_tensor(k_lo[:, :, b * P:(b + 1) * P], src,
                                                      k_hi[:, :, b * P:(b + 1) * P].bitcast(fp32), ALU.subtract)
                    ins.then_inc(tr_out, 1)
                elif kind == "D":
                    b, odd = divmod(s[1], 2)
                    if not odd:
                        continue
                    keys = (b + 1) * P
                    dve.wait_ge(relu_done, L * 4 + s[1] + 1)
                    for h in range(IDX_HEADS):
                        r = probs[:, 2 * b + h % 2, (h // 2) * keys:(h // 2 + 1) * keys]
                        w = w_idx[:, b, h:h + 1]
                        if h == 0:
                            ins = nc.vector.tensor_scalar(score[b][:, :], r, w, None, ALU.mult)
                        else:
                            ins = nc.vector.scalar_tensor_tensor(score[b][:, :], r, w, score[b][:, :], ALU.mult,
                                                                 ALU.add)
                        if h + 1 < IDX_HEADS:
                            link(ins)
                    ins.then_inc(score_done, 1)
                elif kind == "topk":
                    b, r = s[1:]
                    keys = (b + 1) * P
                    if r == 0:
                        dve.wait_ge(score_done, L * 2 + b + 1)
                        link(nc.vector.memset(score[b][0:CHUNK, keys - CHUNK:keys], INADMISSIBLE))
                    link(nc.vector.max(top8[:, :], score[b][:, :]))
                    link(nc.vector.match_replace(score[b][:, :], top8[:, :], score[b][:, :], TAKEN))
                    if r == TOPK // 8 - 1:
                        nc.vector.tensor_scalar(sel_mask[b][:, :], score[b][:, :], TAKEN, NEG, ALU.is_gt, ALU.mult)\
                            .then_inc(mask_done, 1)
                elif kind == "S":
                    i = s[1]
                    g, b, maps, keys = s_task(i)
                    dve.wait_ge(s_done, L * 12 + i + 1)
                    if L * 12 + i >= 2:
                        dve.wait_ge(exp_done, L * 12 + i - 1)
                    nc.vector.tensor_reduce(neg_max[:, i % 2, 0:len(maps)],
                                            sc[i % 2][:, :].rearrange("p (m k) -> p m k", k=keys), AX.X, ALU.max,
                                            negate=True).then_inc(max_done, 1)
                elif kind == "R":
                    i = s[1]
                    g, b, maps, keys = s_task(i)
                    dve.wait_ge(exp_done, L * 12 + i + 1)
                    own = slice(maps[0], maps[-1] + 1, 2)
                    rec = nc.vector.reciprocal(row_rec[:, g, b, own], row_sum[:, g, b, own])
                    if g == 0 and i % 2:
                        link(rec)
                        if L * 3 + i // 2:
                            dve.wait_ge(mix_done, L * 3 + i // 2)
                        for j, m in enumerate(maps):
                            ins = nc.vector.scalar_tensor_tensor(mix_c[:, j:j + 1], row_rec[:, 0, b, m:m + 1],
                                                                 neg_lam[:, :], row_sum[:, 0, b, m - 1:m], ALU.mult,
                                                                 ALU.mult)
                        link(ins)
                        for j in range(len(maps)):
                            p1 = probs[:, (i - 1) % 4, j * keys:(j + 1) * keys]
                            p2 = probs[:, i % 4, j * keys:(j + 1) * keys]
                            ins = nc.vector.scalar_tensor_tensor(p1, p2, mix_c[:, j:j + 1], p1, ALU.mult, ALU.add)
                        ins.then_inc(mix_done, 1)
                    elif g == 1:
                        rec.then_inc(rec_done, 1)
                elif kind == "PV":
                    for g, b, members in PV_GROUP:
                        if g == 1 and s[1] == members[-1]:
                            dve.wait_ge(pv_done, L * 9 + members[-1] + 1)
                            dve.wait_ge(rec_done, L * 6 + (2 if b == 0 else 6))
                            nc.vector.tensor_tensor(
                                y_mix[1][b].rearrange("p j (h d) -> p j h d", d=HEAD),
                                pv[:, :].rearrange("p (j h d) -> p j h d", h=2, d=HEAD),
                                row_rec[:, 1, b, :].rearrange("p (j h) -> p j h", h=2).unsqueeze(3)
                                .to_broadcast([P, 4, 2, HEAD]), ALU.mult)\
                                .then_inc(pv_out, 1)
                elif kind == "hv":
                    b = s[1]
                    dve.wait_ge(sqh_done, L * 2 + b + 1)
                    nc.vector.tensor_scalar(var_h[:, b, :], ssq_h[:, b, :], 1.0 / P, EPS, ALU.mult, ALU.add)\
                        .then_inc(varh_done, 1)
                elif kind == "hn":
                    b = s[1]
                    dve.wait_ge(rstdh_done, L * 2 + b + 1)
                    link(nc.vector.tensor_tensor(scale_h[:, b, :], rstd_h[:, b, :],
                                                 row_rec[:, 0, b, :].rearrange("p (h c) -> p h c", c=2)[:, :, 0],
                                                 ALU.mult))
                    for h in range(B_HEADS):
                        ins = nc.vector.scalar_tensor_tensor(
                            y_mix[0][b][:, h, :], pv[:, h * P:(h + 1) * P],
                            scale_h[:, b, h:h + 1], g_sub[:, :], ALU.mult, ALU.mult)
                    ins.then_inc(pv_out, 1)
                elif kind == "lam":
                    lambda_of(L)
                elif kind == "post0":
                    b, n = s[1:]
                    if n == 0:
                        dve.wait_ge(sq_done[1], L * 4 + 2 * b + 1)
                    else:
                        add_eps(1, L, b, 2)
                    dve.wait_ge(gpost_in, 16 * (L + 1))
                    nc.vector.tensor_tensor(work[:, b, n * N:(n + 1) * N], proj[bank_of("WO", n, b)][:, :],
                                            g_norm[:, n * N:(n + 1) * N], ALU.mult).then_inc(wo_scaled, 1)
                elif kind == "post1":
                    b = s[1]
                    dve.wait_ge(rstd_done[1], L * 2 + b + 1)
                    dve.wait_ge(wo_scaled, L * 4 + 2 * b + 2)
                    nc.vector.scalar_tensor_tensor(resid[:, b, :], work[:, b, :], rstd[:, 1, b:b + 1], resid[:, b, :],
                                                   ALU.mult, ALU.add).then_inc(x1_done, 1)
                elif kind == "ple0":
                    b, n, M = s[1:]
                    half = work[:, b, n * N:(n + 1) * N]
                    dve.wait_ge(wg_sig, M * 4 + 2 * b + n + 1)
                    nc.vector.tensor_tensor(half, half, emb[:, b, n * N:(n + 1) * N], ALU.mult).then_inc(e_done, 1)
                    dve.wait_ge(e_done, M * 4 + 2 * b + n + 1)
                    dve.wait_ge(gple_in, 16 * (M + 1))
                    link(nc.vector.tensor_tensor(e_g[b][:, n * N:(n + 1) * N], half, g_ple[:, n * N:(n + 1) * N],
                                                 ALU.mult))
                elif kind == "ple1":
                    b, M = s[1:]
                    add_eps(2, M, b, 2)
                    dve.wait_ge(rstd_done[2], M * 2 + b + 1)
                    for n in range(2):
                        cols = slice(n * N, (n + 1) * N)
                        nc.vector.scalar_tensor_tensor(resid[:, b, cols], e_g[b][:, cols], rstd[:, 2, b:b + 1],
                                                       resid[:, b, cols], ALU.mult, ALU.add).then_inc(x2_done, 1)

        @block.tensor
        def _(pe):
            def wait_bank(L, chunk, n, b):
                prev = L - 1
                if chunk == "PLE":
                    if L > 0:
                        pe.wait_ge(wg_sig, prev * 4 + (1 if n == 0 else 3) + b)
                elif chunk == "IDX":
                    pe.wait_ge(ple_out, L * 4 + 2 + b + 1)
                elif chunk == "QB":
                    pe.wait_ge(ple_out, L * 4 + b + 1)
                elif chunk == "KB":
                    pe.wait_ge(idx_out, L * 2 + b + 1)
                elif chunk == "VB":
                    pe.wait_ge(z_out, L * 8 + b + 1)
                elif chunk == "QA":
                    pe.wait_ge(z_out, L * 8 + 2 + b + 1)
                elif chunk == "KA":
                    pe.wait_ge(v_out, L * 4 + b + 1)
                elif chunk == "VA":
                    pe.wait_ge(z_out, L * 8 + 4 + b + 1)
                elif chunk == "GA":
                    pe.wait_ge(z_out, L * 8 + 6 + b + 1)
                elif chunk == "GB":
                    pe.wait_ge(v_out, L * 4 + 2 + b + 1)
                elif chunk == "WO":
                    pe.wait_ge(glu_done, L * 4 + 2 * b + n + 1)
                else:
                    pe.wait_ge(wo_scaled, L * 4 + 2 * b + n + 1)

            def wait_tr(L, s):
                i = tr_index(L, s)
                if i > 1:
                    pe.wait_ge(tr_out, i - 1)

            pe.wait_ge(const_done, 2)
            for i in range(WARM[0]):
                nc.tensor.matmul(sc[0][:, 0:P], ident[:, :], ident[:, :], start=True, stop=True)
            for pos, (L, s) in enumerate(STEPS):
                kind = s[0]
                if kind == "mm":
                    u, b = s[1:]
                    g = L * U + u
                    chunk, n, k0, nk, cols = UNITS[u]
                    ps = proj[bank_of(chunk, n, b)][:, 0:cols]
                    if k0 == 0:
                        wait_bank(L, chunk, n, b)
                    pe.wait_ge(lo_done, g + 1)
                    if chunk == "PLE":
                        pe.wait_ge(p_lo_done, L + 1)
                        src_hi, src_lo = p_hi, p_lo
                    else:
                        src = "y" if chunk == "WO" else "x" if chunk == "WG" else "h"
                        pe.wait_ge(at_lo, L * 12 + t8_index(src, b, k0 // 4) + 1)
                        src_hi, src_lo = act_hi, act_lo
                    for k in range(nk):
                        hi = w_hi[:, g % SLOTS, k * cols:(k + 1) * cols]
                        lo = w_lo[:, g % SLOTS, k * cols:(k + 1) * cols]
                        last_k = u == LAST_OF[chunk, n] and k == nk - 1
                        nc.tensor.matmul(ps, src_hi[:, b, k0 + k, :], hi, start=(k0 + k == 0), stop=False)
                        nc.tensor.matmul(ps, src_hi[:, b, k0 + k, :], lo, start=False, stop=False)
                        last = nc.tensor.matmul(ps, src_lo[:, b, k0 + k, :], hi, start=False, stop=last_k)
                    if b == 1:
                        last.then_inc(unit_used, 1)
                    elif last_k:
                        last.then_inc(b0_done, 1)
                elif kind == "pT":
                    m = s[1]
                    pe.wait_ge(p_in[m], 16)
                    if m > 0:
                        pe.wait_ge(pv_out, m * 4)
                    for b in range(NB):
                        for k in range(D_PLE // P):
                            j = b * 2 + k
                            last = nc.tensor.transpose(pv[:, j * P:(j + 1) * P], p_raw[:, b, k * P:(k + 1) * P],
                                                       ident[:, :])
                    last.then_inc(ptr_done, 1)
                    for i in range(WARM[1] if m == 0 else 0):
                        nc.tensor.matmul(sc[0][:, 0:P], ident[:, :], ident[:, :], start=True, stop=True)
                elif kind == "t8":
                    src, b, half = s[1:]
                    i = t8_index(src, b, half)
                    if src == "h":
                        pe.wait_ge(h_done, L * 2 + b + 1)
                    elif src == "y":
                        pe.wait_ge(y_done, L * 4 + 2 + b + 1)
                    else:
                        pe.wait_ge(x1_done, L * 2 + b + 1)
                    if i in (4, 5):
                        pe.wait_ge(exp_done, L * 12 + 7 + i)
                    elif L * 12 + i >= 2:
                        pe.wait_ge(at_lo, L * 12 + i - 1)
                    for j in range(4):
                        k = 4 * half + j
                        if src == "h":
                            tile = work[:, b, k * P:(k + 1) * P]
                        elif src == "y":
                            tile = y_mix[1 - half][b][:, j, :]
                        else:
                            tile = resid[:, b, k * P:(k + 1) * P]
                        last = nc.tensor.transpose(sc[half][:, j * P:(j + 1) * P], tile, ident[:, :])
                    last.then_inc(t8_done, 1)
                elif kind == "TI":
                    b = s[1]
                    wait_tr(L, s)
                    pe.wait_ge(rope_idx, L * 2 + b + 1)
                    for j in range(3):
                        last = nc.tensor.transpose(tr[:, j * P:(j + 1) * P], z_idx[:, b, j * P:(j + 1) * P],
                                                   ident[:, :])
                    last.then_inc(tr_done, 1)
                elif kind == "T":
                    chunk, b = s[1:]
                    wait_tr(L, s)
                    pe.wait_ge(rope_z, L * 8 + Z_ORDER.index(chunk) * 2 + b + 1)
                    z = z_view(chunk, b)
                    for j in range(4):
                        last = nc.tensor.transpose(tr[:, j * P:(j + 1) * P], z[:, j * P:(j + 1) * P], ident[:, :])
                    last.then_inc(tr_done, 1)
                elif kind == "D":
                    i = s[1]
                    b, odd = divmod(i, 2)
                    keys = (b + 1) * P
                    pe.wait_ge(tr_out, tr_index(L, ("TI", b)))
                    if i < 2:
                        pe.wait_ge(at_lo, L * 12 + 3 + i)
                    else:
                        pe.wait_ge(relu_done, L * 4 + i - 1)
                    rows = slice(odd * HEAD, (odd + 1) * HEAD)
                    for j in range(2):
                        last = nc.tensor.matmul(sc[i % 2][:, j * keys:(j + 1) * keys],
                                                idxT[rows, j, b * P:(b + 1) * P], idxT[rows, 2, 0:keys],
                                                start=True, stop=True)
                    last.then_inc(dots_done, 1)
                elif kind == "S":
                    i = s[1]
                    g, b, maps, keys = s_task(i)
                    keys_from = ("KB" if g == 0 else "KA", b)
                    if b == 0:
                        pe.wait_ge(qk_hi_done, L * 6 + QK_SPLIT.index(keys_from) + 1)
                    else:
                        pe.wait_ge(tr_out, tr_index(L, ("T",) + keys_from))
                    if i < 2:
                        pe.wait_ge(relu_done, L * 4 + 3 + i)
                    else:
                        pe.wait_ge(exp_done, L * 12 + i - 1)
                    if g == 1:
                        pe.wait_ge(mask_done, L * 2 + b + 1)
                        mask, first = sel_mask[b], 0
                    else:
                        mask, first = causal, keys - CHUNK
                    for j, m in enumerate(maps):
                        rows = slice((m % 2) * HEAD, (m % 2 + 1) * HEAD)
                        ps = sc[i % 2][:, j * keys:(j + 1) * keys]
                        if b == 0:
                            nc.tensor.matmul(ps, qT[g][rows, m // 2, 0:P], kT[rows, m // 2, :], start=True, stop=False)
                        else:
                            qh, ql = q_hi[rows, m // 2, :], q_lo[rows, m // 2, :]
                            kh, kl = k_hi[rows, m // 2, :], k_lo[rows, m // 2, :]
                            nc.tensor.matmul(ps, qh, kh, start=True, stop=False)
                            nc.tensor.matmul(ps, qh, kl, start=False, stop=False)
                            nc.tensor.matmul(ps, ql, kh, start=False, stop=False)
                        last = nc.tensor.matmul(ps[:, first:keys], ident16[:, :], mask[:, 0:keys - first],
                                                start=False, stop=True)
                    last.then_inc(s_done, 1)
                elif kind == "PT":
                    n = s[1]
                    g, b, tiles = pt_task(n)
                    wait_tr(L, s)
                    if g == 0:
                        pe.wait_ge(mix_done, L * 3 + n + 1)
                    else:
                        pe.wait_ge(exp_done, L * 12 + tiles[0][2] + 1)
                    for j, (h, kt, si, col) in enumerate(tiles):
                        last = nc.tensor.transpose(tr[:, j * P:(j + 1) * P], probs[:, si % 4, col:col + P],
                                                   ident[:, :])
                    last.then_inc(tr_done, 1)
                elif kind == "PV":
                    n = s[1]
                    g, b, tiles = pt_task(n)
                    width = P if g == 0 else HEAD
                    pe.wait_ge(tr_out, tr_index(L, ("PT", n)))
                    pe.wait_ge(v_out, L * 4 + 2 * g + b + 1)
                    if n == 0:
                        pe.wait_ge(p_lo_done, L + 1)
                    for gi, (_, _, members) in enumerate(PV_GROUP):
                        if gi and n == members[0]:
                            pe.wait_ge(pv_out, L * 4 + gi)
                    for j, (h, kt, si, col) in enumerate(tiles):
                        last = nc.tensor.matmul(pv[:, h * width:(h + 1) * width], pT[:, n % 3, j, :],
                                                v_all[:, kt, g, h * width:(h + 1) * width], start=(kt == 0),
                                                stop=(kt == b))
                    last.then_inc(pv_done, 1)


_INS = ["x", "p", "pre_norm_g", "w_in", "w_out", "post_norm_g", "lambda_q1", "lambda_k1", "lambda_q2", "lambda_k2",
        "subln_g", "w_ple_gate", "w_ple_proj", "ple_norm_g"]


def kernel(**inputs):
    import numpy as _np
    import concourse.bacc as _bacc
    from concourse import mybir as _mybir
    from concourse.bass_utils import run_bass_kernel_spmd as _run

    nc = _bacc.Bacc("TRN2", target_bir_lowering=False, num_devices=1)
    arrays, args = {}, []
    for name in _INS:
        a = _np.ascontiguousarray(inputs[name])
        arrays[f"in_{name}_dram"] = a
        args.append(nc.dram_tensor(f"in_{name}_dram", a.shape, _mybir.dt.from_np(a.dtype), kind="ExternalInput").ap())
    f32 = _np.float32
    inv = f32(500000.0) ** (-_np.arange(0, ROT, 2, dtype=f32) / f32(ROT))
    angle = _np.arange(SEQ, dtype=f32)[:, None] * inv[None, :]
    table = _np.concatenate([_np.cos(angle), _np.cos(angle), -_np.sin(angle), _np.sin(angle)], axis=1).astype(f32)
    arrays["rope_dram"] = table
    args.append(nc.dram_tensor("rope_dram", table.shape, _mybir.dt.float32, kind="ExternalInput").ap())
    args.append(nc.dram_tensor("out_0_dram", (1, SEQ, D_MODEL), _mybir.dt.float32, kind="ExternalOutput").ap())
    build(nc, *args)
    r = _run(nc, [arrays], core_ids=[0])
    return r.results[0]["out_0_dram"]
```
